# Optimizing a Trainium2 kernel written in Bass

```python
import jax, jax.numpy as jnp
from jax import lax
import numpy as np

D_MODEL = 1024
BATCH = 1
SEQ = 512
DEPTH = 2

CHUNK = 64
Q_BLOCK = 128
N_A_LAYERS = DEPTH // 2
N_B_LAYERS = DEPTH - N_A_LAYERS
SB_HEADS = 16
SB_HEAD_DIM = D_MODEL // SB_HEADS
MLA_HEADS = 16
MLA_NOPE_DIM = 64
MLA_ROPE_DIM = 32
MLA_V_DIM = 64
MLA_Q_RANK = 384
MLA_KV_RANK = 256
D_FF = 4 * D_MODEL
ROPE_THETA = 10000.0
NORM_EPS = 1e-6
MAX_POS_OFFSET = 4096

kernel_name = "yoco_stickbreak_mla_hybrid"

def rms_norm(x, g):
    xf = x.astype(jnp.float32)
    y = xf * lax.rsqrt(jnp.mean(xf * xf, axis=-1, keepdims=True) + NORM_EPS)
    return (y * g.astype(jnp.float32)).astype(x.dtype)

def rope_tables(positions):
    inv_freq = ROPE_THETA ** (-jnp.arange(0, MLA_ROPE_DIM, 2, dtype=jnp.float32) / MLA_ROPE_DIM)
    ang = positions.astype(jnp.float32)[..., None] * inv_freq
    return jnp.cos(ang), jnp.sin(ang)

def apply_rope(t, cos, sin):
    half = MLA_ROPE_DIM // 2
    t1 = t[..., :half].astype(jnp.float32)
    t2 = t[..., half:].astype(jnp.float32)
    out = jnp.concatenate([t1 * cos - t2 * sin, t2 * cos + t1 * sin], axis=-1)
    return out.astype(t.dtype)

def to_query_blocks(t):
    b, s, h, d = t.shape
    return t.reshape(b, s // Q_BLOCK, Q_BLOCK, h, d).transpose(1, 0, 3, 2, 4)

def from_query_blocks(t):
    nb, b, qb, h, d = t.shape
    return t.transpose(1, 0, 2, 3, 4).reshape(b, nb * qb, h * d)

def stick_breaking_attention(h, w_qkv, w_o):
    b, s, _ = h.shape
    qkv = (h @ w_qkv).reshape(b, s, 3, SB_HEADS, SB_HEAD_DIM)
    q, k, v = qkv[:, :, 0], qkv[:, :, 1], qkv[:, :, 2]
    k_h = k.transpose(0, 2, 1, 3)
    v_h = v.transpose(0, 2, 1, 3)
    q_blocks = to_query_blocks(q)
    scale = SB_HEAD_DIM ** -0.5
    key_pos = jnp.arange(s)

    def block(args):
        q_blk, blk_idx = args
        q_pos = blk_idx * Q_BLOCK + jnp.arange(Q_BLOCK)
        z = jnp.einsum('bhqd,bhkd->bhqk', q_blk, k_h).astype(jnp.float32) * scale
        causal = key_pos[None, :] < q_pos[:, None]
        log_beta = jax.nn.log_sigmoid(z)
        log_keep = jnp.where(causal, jax.nn.log_sigmoid(-z), 0.0)
        shifted = jnp.concatenate([log_keep[..., 1:], jnp.zeros_like(log_keep[..., :1])], axis=-1)
        log_survive = lax.cumsum(shifted, axis=3, reverse=True)
        weights = jnp.where(causal, jnp.exp(log_beta + log_survive), 0.0)
        return jnp.einsum('bhqk,bhkd->bqhd', weights.astype(v_h.dtype), v_h)

    out = lax.map(block, (q_blocks, jnp.arange(s // Q_BLOCK)))
    return from_query_blocks(out) @ w_o

def mla_shared_kv(h, w_dkv, kv_lat_norm, w_ukv, cos, sin):
    b, s, _ = h.shape
    down = h @ w_dkv
    c_kv = rms_norm(down[..., :MLA_KV_RANK], kv_lat_norm)
    k_rope = apply_rope(down[..., MLA_KV_RANK:], cos, sin)
    kv = (c_kv @ w_ukv).reshape(b, s, MLA_HEADS, MLA_NOPE_DIM + MLA_V_DIM)
    k_nope = kv[..., :MLA_NOPE_DIM].transpose(0, 2, 1, 3)
    v = kv[..., MLA_NOPE_DIM:].transpose(0, 2, 1, 3)
    return k_nope, k_rope, v

def mla_attention(h, w_dq, q_lat_norm, w_uq, w_o, k_nope, k_rope, v, cos, sin):
    b, s, _ = h.shape
    c_q = rms_norm(h @ w_dq, q_lat_norm)
    q = (c_q @ w_uq).reshape(b, s, MLA_HEADS, MLA_NOPE_DIM + MLA_ROPE_DIM)
    q_nope = q[..., :MLA_NOPE_DIM]
    q_rope = apply_rope(q[..., MLA_NOPE_DIM:], cos[:, :, None, :], sin[:, :, None, :])
    qn_blocks = to_query_blocks(q_nope)
    qr_blocks = to_query_blocks(q_rope)
    scale = (MLA_NOPE_DIM + MLA_ROPE_DIM) ** -0.5
    key_chunk = jnp.arange(s) // CHUNK

    def block(args):
        qn, qr, blk_idx = args
        q_chunk = (blk_idx * Q_BLOCK + jnp.arange(Q_BLOCK)) // CHUNK
        scores = (jnp.einsum('bhqd,bhkd->bhqk', qn, k_nope)
                  + jnp.einsum('bhqr,bkr->bhqk', qr, k_rope)).astype(jnp.float32) * scale
        allowed = key_chunk[None, :] <= q_chunk[:, None]
        probs = jax.nn.softmax(jnp.where(allowed, scores, -jnp.inf), axis=-1)
        return jnp.einsum('bhqk,bhkd->bqhd', probs.astype(v.dtype), v)

    out = lax.map(block, (qn_blocks, qr_blocks, jnp.arange(s // Q_BLOCK)))
    return from_query_blocks(out) @ w_o

def squared_relu_mlp(h, w1, w2):
    return jnp.square(jax.nn.relu(h @ w1)) @ w2

def setup_inputs(seed: int = 0) -> dict:
    key = jax.random.key(seed)
    ks = jax.random.split(key, 20)

    def w(k, shape, fan_in, gain=1.0):
        return jax.random.normal(k, shape, jnp.float32) * (gain * fan_in ** -0.5)

    def gains(k, shape):
        return 1.0 + 0.02 * jax.random.normal(k, shape, jnp.float32)

    out_gain = (2.0 * DEPTH) ** -0.5
    x = jax.random.normal(ks[0], (BATCH, SEQ, D_MODEL), jnp.float32)
    offsets = jax.random.randint(ks[1], (BATCH, 1), 0, MAX_POS_OFFSET, dtype=jnp.int32)
    positions = offsets + jnp.arange(SEQ, dtype=jnp.int32)[None, :]
    return {
        "x": x,
        "positions": positions,
        "attn_norm": gains(ks[2], (DEPTH, D_MODEL)),
        "mlp_norm": gains(ks[3], (DEPTH, D_MODEL)),
        "sb_w_qkv": w(ks[4], (N_A_LAYERS, D_MODEL, 3 * D_MODEL), D_MODEL),
        "sb_w_o": w(ks[5], (N_A_LAYERS, D_MODEL, D_MODEL), D_MODEL, out_gain),
        "kv_norm": gains(ks[6], (D_MODEL,)),
        "mla_w_dkv": w(ks[7], (D_MODEL, MLA_KV_RANK + MLA_ROPE_DIM), D_MODEL),
        "mla_kv_lat_norm": gains(ks[8], (MLA_KV_RANK,)),
        "mla_w_ukv": w(ks[9], (MLA_KV_RANK, MLA_HEADS * (MLA_NOPE_DIM + MLA_V_DIM)), MLA_KV_RANK),
        "mla_w_dq": w(ks[10], (N_B_LAYERS, D_MODEL, MLA_Q_RANK), D_MODEL),
        "mla_q_lat_norm": gains(ks[11], (N_B_LAYERS, MLA_Q_RANK)),
        "mla_w_uq": w(ks[12], (N_B_LAYERS, MLA_Q_RANK, MLA_HEADS * (MLA_NOPE_DIM + MLA_ROPE_DIM)), MLA_Q_RANK),
        "mla_w_o": w(ks[13], (N_B_LAYERS, MLA_HEADS * MLA_V_DIM, D_MODEL), MLA_HEADS * MLA_V_DIM, out_gain),
        "mlp_w1": w(ks[14], (DEPTH, D_MODEL, D_FF), D_MODEL),
        "mlp_w2": w(ks[15], (DEPTH, D_FF, D_MODEL), D_FF, out_gain),
        "final_norm": gains(ks[16], (D_MODEL,)),
    }

def reference(x, positions, attn_norm, mlp_norm, sb_w_qkv, sb_w_o, kv_norm, mla_w_dkv,
              mla_kv_lat_norm, mla_w_ukv, mla_w_dq, mla_q_lat_norm, mla_w_uq, mla_w_o,
              mlp_w1, mlp_w2, final_norm):
    cos, sin = rope_tables(positions)
    k_nope = k_rope = v = None
    for layer in range(DEPTH):
        if layer < N_A_LAYERS:
            x = x + stick_breaking_attention(rms_norm(x, attn_norm[layer]),
                                             sb_w_qkv[layer], sb_w_o[layer])
        else:
            if layer == N_A_LAYERS:
                k_nope, k_rope, v = mla_shared_kv(rms_norm(x, kv_norm), mla_w_dkv,
                                                  mla_kv_lat_norm, mla_w_ukv, cos, sin)
            j = layer - N_A_LAYERS
            x = x + mla_attention(rms_norm(x, attn_norm[layer]), mla_w_dq[j], mla_q_lat_norm[j],
                                  mla_w_uq[j], mla_w_o[j], k_nope, k_rope, v, cos, sin)
        x = x + squared_relu_mlp(rms_norm(x, mlp_norm[layer]), mlp_w1[layer], mlp_w2[layer])
    return rms_norm(x, final_norm)


_drawn_inputs = setup_inputs


def setup_inputs(seed=0):
    import zlib

    import numpy as np

    out = dict(_drawn_inputs(seed))
    spreads = {}
    factors = {'attn_norm': 6.981,
     'mlp_norm': 3.708,
     'kv_norm': 8.0,
     'mla_kv_lat_norm': 8.0,
     'mla_q_lat_norm': 8.0,
     'final_norm': 2.855}
    for name, (base, spread) in spreads.items():
        noise = np.random.default_rng([zlib.crc32(name.encode()), seed]).standard_normal(out[name].shape)
        drawn = base * np.exp(spread * noise) if base else spread * noise
        out[name] = __import__('jax').numpy.asarray(drawn.astype(out[name].dtype))
    for name, factor in factors.items():
        out[name] = (out[name] * factor).astype(out[name].dtype)
    return out
```

```python
from contextlib import ExitStack

import numpy as np

import concourse.bass as bass
from concourse import mybir

F32 = mybir.dt.float32
F32R = mybir.dt.float32r
BF16 = mybir.dt.bfloat16
I32 = mybir.dt.int32
ACT = mybir.ActivationFunctionType
ALU = mybir.AluOpType
AX = mybir.AxisListType

P = 128
D = 1024
T = 512
KT = D // P
TT = T // P
FF = 4096
FB = 1024
NFB = FF // FB
HD = 64
NH = 16
HALF = 8
PAIRS = HALF // 2
ROPE = 32
NOPE = 64
QH = NOPE + ROPE
QR = 384
KR = 256
QRT = QR // P
KRT = KR // P
EPS = 1e-6
SB_SCALE = HD ** -0.5
MLA_SCALE = QH ** -0.5
SLAB = 2048
MASKED = -1e30

OFF = (0, 512, 1024, 896)
WID = tuple(T - P * j for j in range(TT))
PACK = sum(WID)

TWO_PI = 6.283185307179586
PI_A = 6.28125
PI_B = float(np.float32(np.float32(TWO_PI - PI_A).view(np.uint32).__and__(np.uint32(0xFFFFF000)).view(np.float32)))
PI_C = TWO_PI - PI_A - PI_B
ROUNDER = 1.5 * 2.0 ** 23
PI_SAFE = 3.1415925

C_IDENT, C_SWAP, C_TRI, C_ONES, C_NEGC, C_NEGM = range(6)
COL_FREQ, COL_COS, COL_SIN, COL_ONE = range(4)
G_ATTN, G_MLP, G_KV, G_FIN, G_LKV, G_LQ, G_END = 0, 16, 32, 40, 48, 50, 53

N_SB = 0
SB_SLABS = 6
N_SBO = N_SB + 2 * SB_SLABS
N_MLP0 = N_SBO + 4
MLP_SLABS = 8
N_DOWN = N_MLP0 + NFB * MLP_SLABS
N_MLA = N_DOWN + 4
MLA_SLABS = 4
N_MLAO = N_MLA + 2 * MLA_SLABS
N_MLP1 = N_MLAO + 4


def constants():
    c = np.zeros((P, 6 * P + 4), np.float32)
    k, q = np.arange(P)[:, None], np.arange(P)[None, :]
    m = [c[:, n * P:(n + 1) * P] for n in range(6)]
    m[C_IDENT][:] = k == q
    half = ROPE // 2
    m[C_SWAP][:] = 1.0 * ((q % ROPE >= half) & (k == q - half)) - 1.0 * ((q % ROPE < half) & (k == q + half))
    m[C_TRI][:] = -1.0 * (k >= q)
    m[C_ONES][:] = -1.0
    m[C_NEGC][:] = MASKED * (k >= q)
    m[C_NEGM][:] = MASKED * (k // 64 < q // 64)
    col = c[:, 6 * P:]
    freq = np.float32(10000.0) ** (-np.arange(0, ROPE, 2, dtype=np.float32) / np.float32(ROPE))
    row = np.arange(P)
    col[:, COL_FREQ] = freq[row % half]
    col[:, COL_COS] = MLA_SCALE * ((row >= 64) & (row < 96))
    col[:, COL_SIN] = MLA_SCALE * (1.0 * (row >= 112) - 1.0 * ((row >= 96) & (row < 112)))
    col[:, COL_ONE] = MLA_SCALE * (row < 64)
    return c



SB_GROUPS = 1 + TT + 2 * PAIRS
MLP_GROUPS = 4 * KT // 2
MLA_GROUPS = 1 + TT + 3 * PAIRS
G_SB = 2
G_SBO = G_SB + 2 * SB_GROUPS
G_MLP0 = G_SBO + KT
G_DOWN = G_MLP0 + NFB * MLP_GROUPS
G_MLA = G_DOWN + KRT + 1 + QRT
G_MLAO = G_MLA + 2 * MLA_GROUPS
G_MLP1 = G_MLAO + KT


def sb_group(kind, n=0):
    return {"v_first": 1, "v": 2 + n, "q": TT + 2 + 2 * n, "k": TT + 3 + 2 * n}[kind]


def mla_group(kind, n=0):
    return {"v_first": 1, "v": 2 + n, "k": TT + 2 + 3 * n, "q": TT + 3 + 3 * (n // 2) + n % 2}[kind]


def build(nc, x_in, pos_in, attn_norm, mlp_norm, w_qkv, w_o, kv_norm, w_dkv, kv_lat, w_ukv, w_dq, q_lat, w_uq,
          mla_wo, w1, w2, final_norm, consts, out):
    with ExitStack() as ctx:
        def sb(name, shape, dt):
            return ctx.enter_context(nc.sbuf_tensor(name, shape, dt))

        names = """const_in gain_in pos_landed const_cast slab_asked slab_begun slab_hi slab_hi_act slab_split group
            xt_ready x_done h_hi h_lo sq_done acc_add gq_hi gq_lo
            st_ps st_var st_sqrt st_inv q_scale
            v_hi v_lo z_rdy z_abs sp_exp sp_ln sp_sum sp_hi sp_lo surv_rdy w_exp w_hi w_lo pv_rdy
            o_tmp o_add o_hi o_lo q_t q_hi q_lo k_t k_hi k_lo so_x
            rope_pos rope_ps rope_v rope_s
            lat_u lat_sq lat_add lat_hi lat_lo ra_u rb_ps kr_v kr_hi kr_lo tab_v
            mv_hi mv_lo mz_rdy m_max m_exp m_norm mt_rdy mw_hi mw_lo mpv_rdy mo_tmp mo_add mo_hi mo_lo
            mq_t mq_hi mq_lo mk_t mk_hi mk_lo mo_x
            f_xg f_tr f_out_v f_out_s out_done""".split()
        s = {n: ctx.enter_context(nc.semaphore(n)) for n in names}
        x_landed = [ctx.enter_context(nc.semaphore(f"x_landed{t}")) for t in range(TT)]
        raw_landed = [ctx.enter_context(nc.semaphore(f"raw_landed{b}")) for b in range(2)]
        mlp_s = [{n: ctx.enter_context(nc.semaphore(f"mlp{l}_{n}")) for n in "evac sq hi lo".split()}
                 for l in range(2)]
        group = s["group"]

        xT = sb("xT", [P, KT, T], F32)
        h_hi, h_lo = sb("h_hi", [P, KT, T], F32R), sb("h_lo", [P, KT, T], F32R)
        u_hi, u_lo = sb("u_hi", [P, KT, T], F32R), sb("u_lo", [P, KT, T], F32R)
        raw = [sb(f"raw{b}", [P, SLAB], F32) for b in range(2)]
        w_hi = [sb(f"w_hi{b}", [P, SLAB], F32R) for b in range(2)]
        w_lo = [sb(f"w_lo{b}", [P, SLAB], F32R) for b in range(2)]
        vst = sb("vst", [P, TT, HALF, 2, HD], F32R)
        qop = sb("qop", [P, 2, 2, T], F32R)
        kop = sb("kop", [P, 2, 2, T], F32R)
        pr_hi = [sb(f"pr_hi{b}", [P, PACK], F32R) for b in range(2)]
        pr_lo = [sb(f"pr_lo{b}", [P, PACK], F32R) for b in range(2)]
        scr = sb("scr", [P, 8, T], F32)
        r_tok = sb("r_tok", [P, T], F32)
        tab_a = sb("tab_a", [P, T], F32)
        tab_b = sb("tab_b", [P, T], F32)
        acc = sb("acc", [P, T], F32)
        ident = sb("ident", [P, P], F32)
        swap = sb("swap", [P, P], F32)
        ones = sb("ones", [P, P], F32)
        tri_r, ones_r = sb("tri_r", [P, P], F32R), sb("ones_r", [P, P], F32R)
        ident_b, negc_b, negm_b = (sb(n, [P, P], BF16) for n in ("ident_b", "negc_b", "negm_b"))
        cols = sb("cols", [P, 4], F32)
        gain = sb("gain", [P, G_END], F32)
        r_col = sb("r_col", [P, TT], F32)
        nmax = sb("nmax", [P, 2, TT], F32)
        rsum = sb("rsum", [P, 2, TT], F32)

        zb = ctx.enter_context(nc.psum_tensor("zb", [P, 6, T], F32))
        pj = ctx.enter_context(nc.psum_tensor("pj", [P, T], F32))
        po = ctx.enter_context(nc.psum_tensor("po", [P, T], F32))
        zf = zb[:].rearrange("p b t -> p (b t)")
        banks = [zb[:, b, :] for b in range(6)] + [pj[:], po[:]]

        scf = scr[:].rearrange("p a t -> p (a t)")
        prob = [scf[:, b * PACK:(b + 1) * PACK] for b in range(2)]
        t_proj, t_half, t_out = scr[:, 5, :], scr[:, 6, :], scr[:, 7, :]
        sq_tmp = [tab_a, tab_b]
        cos_t, sin_t = scr[:, 0, :], scr[:, 1, :]

        def z_of(g):
            return zf[:, (g % 2) * 3 * T:(g % 2) * 3 * T + PACK]

        def gcol(n):
            return gain[:, n:n + 1]

        def start_at_one(engine, which):
            for n in which.split():
                engine.sem_inc(s[n], 1)

        block = ctx.enter_context(nc.Block())

        @block.sync
        def _(sp):
            for t in range(TT):
                sp.dma_start(scf[:, t * D:(t + 1) * D], x_in[0, t * P:(t + 1) * P, :]).then_inc(x_landed[t], 16)

            def slab(base_n, j, puts, it=0, per=0):
                sp.wait_ge(s["slab_split"], it * per + (base_n + j + 1))
                sp.sem_inc(s["slab_asked"], 1)
                for dst, src in puts:
                    sp.dma_start(dst(raw[j % 2]), src).then_inc(raw_landed[j % 2], 16)

            def tiles(src, r0, rows, c0, width):
                kt = rows // P // 2
                return [(lambda r, n=n: r[:, 0:2 * kt * width].rearrange("p (k c) -> p k c", c=width)[
                            :, n * kt:(n + 1) * kt, :],
                         src[bass.ds(r0 + n * kt * P, kt * P), bass.ds(c0, width)].rearrange(
                             "(k p) c -> p k c", p=P)) for n in range(2)]

            wq = w_qkv[0]
            with sp.Fori(0, 2) as i:
                for n in range(2):
                    slab(N_SB, n, tiles(wq, n * T, T, i * T + 2 * D, T), i, SB_SLABS)
                for quad in range(2):
                    for which in range(2):
                        slab(N_SB, 2 + 2 * quad + which, tiles(wq, 0, D, i * T + (quad * 256 + which * D), 256),
                             i, SB_SLABS)
            for j in range(4):
                slab(N_SBO, j, tiles(w_o[0], 0, D, 256 * j, 256))

            def mlp(layer, base_n):
                with sp.Fori(0, NFB) as i:
                    for j in range(4):
                        slab(base_n, j, tiles(w1[layer], 0, D, i * FB + 256 * j, 256), i, MLP_SLABS)
                    for j in range(4):
                        slab(base_n, 4 + j, tiles(w2[layer], i * FB, FB, 256 * j, 256), i, MLP_SLABS)

            mlp(0, N_MLP0)
            slab(N_DOWN, 0, tiles(w_dkv, 0, D, 0, KR))
            slab(N_DOWN, 1, tiles(w_dkv, 0, D, KR, ROPE))
            slab(N_DOWN, 2, tiles(w_dq[0], 0, D, 0, 256))
            slab(N_DOWN, 3, tiles(w_dq[0], 0, D, 256, P))
            ukv = w_ukv.rearrange("(k p) (h c) -> k p h c", p=P, c=P)
            uq = w_uq[0].rearrange("(k p) (h c) -> k p h c", p=P, c=QH)
            with sp.Fori(0, 2) as i:
                for kt in range(KRT):
                    slab(N_MLA, kt, [
                        (lambda r, n=n: r[:, 256 * n:256 * (n + 1)].rearrange("p (h c) -> p h c", c=HD),
                         ukv[kt, :, bass.ds(i * HALF + 4 * n, 4), HD:P]) for n in range(2)], i, MLA_SLABS)
                for quad in range(2):
                    slab(N_MLA, 2 + quad, [
                        (lambda r, kt=kt: r[:, 4 * QH * kt:4 * QH * (kt + 1)].rearrange("p (h c) -> p h c", c=QH),
                         uq[kt, :, bass.ds(i * HALF + 4 * quad, 4), :]) for kt in range(QRT)] + [
                        (lambda r, kt=kt: r[:, 1536 + 256 * kt:1536 + 256 * (kt + 1)].rearrange(
                            "p (h c) -> p h c", c=HD),
                         ukv[kt, :, bass.ds(i * HALF + 4 * quad, 4), 0:HD]) for kt in range(KRT)], i, MLA_SLABS)
            for j in range(4):
                slab(N_MLAO, j, tiles(mla_wo[0], 0, D, 256 * j, 256))
            mlp(1, N_MLP1)
            for t in range(TT):
                sp.wait_ge(s["f_out_v"], t + 1)
                sp.wait_ge(s["f_out_s"], t + 1)
                sp.dma_start(out[0, t * P:(t + 1) * P, :], scf[:, t * D:(t + 1) * D]).then_inc(s["out_done"], 16)
            sp.wait_ge(s["out_done"], 16 * TT)

        IN_MLA = N_MLA
        IN_MLA_IT = 2 + QRT + KRT
        IN_MLAO = IN_MLA + 2 * IN_MLA_IT
        IN_MLP1 = IN_MLAO + 4
        HI_OUT0 = 0
        HI_MLP0 = 2
        HI_DOWN = HI_MLP0 + NFB * MLP_SLABS
        HI_OUT1 = HI_DOWN + 3 + 4
        HI_MLP1 = HI_OUT1 + 2

        def full(width):
            return [(lambda w: w[:, 0:width], lambda w: w[:, 0:width])]

        rope_parts = [((lambda w, r=r: w[:, 0:KT * P].rearrange("p (k r c) -> p k r c", k=KT, r=4)[:, :, r, :]),
                       (lambda w: w[:, 0:KT * ROPE].rearrange("p (k c) -> p k c", k=KT))) for r in range(4)]

        @block.gpsimd
        def _(gp):
            gp.dma_start(ident[:], consts[:, C_IDENT * P:(C_IDENT + 1) * P]).then_inc(s["const_in"], 16)
            gp.dma_start(swap[:], consts[:, C_SWAP * P:(C_SWAP + 1) * P]).then_inc(s["const_in"], 16)
            gp.dma_start(r_tok[:], consts[:, C_TRI * P:(C_NEGM + 1) * P]).then_inc(s["const_in"], 16)
            gp.dma_start(cols[:], consts[:, 6 * P:6 * P + 4]).then_inc(s["const_in"], 16)
            gp.sem_inc(s["slab_split"], 1)
            gp.sem_inc(group, 2)
            gp.memset(ones[:], 1.0).then_inc(s["const_cast"], 1)
            gp.wait_ge(s["const_in"], 64)
            gp.tensor_copy(tri_r[:], r_tok[:, 0:P]).then_inc(s["slab_split"], 1)
            gp.tensor_copy(ones_r[:], r_tok[:, P:2 * P]).then_inc(s["const_cast"], 1)
            gp.tensor_copy(negc_b[:], r_tok[:, 2 * P:3 * P]).then_inc(s["const_cast"], 1)
            gp.tensor_copy(negm_b[:], r_tok[:, 3 * P:4 * P]).then_inc(s["const_cast"], 1)
            gp.tensor_copy(ident_b[:], ident[:]).then_inc(s["const_cast"], 1)

            def split(b, landed, used, seen, parts):
                gp.wait_ge(raw_landed[b], landed)
                gp.wait_ge(group, used)
                gp.sem_inc(s["slab_begun"], 1)
                for to, frm in parts:
                    gp.tensor_copy(to(w_hi[b]), frm(raw[b])).then_inc(s["slab_hi"], 1)
                gp.wait_ge(s["slab_hi"], seen + len(parts))
                for to, frm in parts:
                    ins = gp.tensor_tensor(to(w_lo[b]), frm(raw[b]), to(w_hi[b]).bitcast(F32), ALU.subtract)
                ins.then_inc(s["slab_split"], 1)

            def split_lo(b, seen, parts):
                gp.wait_ge(s["slab_hi_act"], seen)
                for to, frm in parts:
                    ins = gp.tensor_tensor(to(w_lo[b]), frm(raw[b]), to(w_hi[b]).bitcast(F32), ALU.subtract)
                ins.then_inc(s["slab_split"], 1)

            last = [sb_group("v_first"), sb_group("v", TT - 1), sb_group("q", 1), sb_group("k", 1),
                    sb_group("q", 3), sb_group("k", 3)]
            with gp.Fori(0, 2) as i:
                for j in range(SB_SLABS):
                    used = last[j - 2] if j >= 2 else last[j + 4] - SB_GROUPS
                    split(j % 2, i * (16 * SB_SLABS) + 32 * (j // 2 + 1), i * SB_GROUPS + (G_SB + used),
                          i * SB_SLABS + j, full(SLAB))
            def out_slabs(n_in, g0, seen, hi0):
                for j in range(4):
                    if j < 2:
                        split(j, 16 * n_in + 32, g0 - 1 + j, seen + j, full(SLAB))
                    else:
                        split_lo(j % 2, hi0 + j - 1, full(SLAB))

            def mlp_slabs(hi0):
                with gp.Fori(0, NFB) as i:
                    for j in range(MLP_SLABS):
                        split_lo(j % 2, i * MLP_SLABS + (hi0 + j + 1), full(SLAB))

            seen = 2 * SB_SLABS
            out_slabs(N_SBO, G_SBO, seen, HI_OUT0)
            seen += 2
            mlp_slabs(HI_MLP0)
            for j, (done, parts) in enumerate(((1, full(SLAB)), (5, rope_parts), (6, full(SLAB)), (7, full(KT * P)))):
                split_lo(j % 2, HI_DOWN + done, parts)

            def head_cols(c0, c1, width):
                return lambda w: w[:, 0:QRT * 4 * width].rearrange("p (k h c) -> p k h c", k=QRT, h=4)[:, :, :, c0:c1]

            half = ROPE // 2
            qk_parts = [(head_cols(0, QH, P), head_cols(0, QH, QH)),
                        (head_cols(QH, QH + half, P), head_cols(NOPE + half, QH, QH)),
                        (head_cols(QH + half, P, P), head_cols(NOPE, NOPE + half, QH)),
                        (lambda w: w[:, 1536:2048], lambda w: w[:, 1536:2048])]
            per_it = 2 + 2 * len(qk_parts)
            with gp.Fori(0, 2) as i:
                for j in range(2):
                    split(j, i * (16 * IN_MLA_IT) + 16 * (IN_MLA + 2), i * MLA_GROUPS + (G_MLA - 1 + j),
                          i * per_it + (seen + j), full(T))
                for quad in range(2):
                    used = mla_group("v_first") if quad == 0 else mla_group("v", TT - 1)
                    split(quad, i * (16 * IN_MLA_IT) + 16 * (IN_MLA + IN_MLA_IT), i * MLA_GROUPS + (G_MLA + used),
                          i * per_it + (seen + 2 + len(qk_parts) * quad), qk_parts)
            seen += 2 * per_it
            out_slabs(IN_MLAO, G_MLAO, seen, HI_OUT1)
            mlp_slabs(HI_MLP1)

        @block.tensor
        def _(pe):
            def mm3(o, l, r, start, stop, check=False):
                nc.tensor.matmul(o, l[0], r[0], start=start, stop=False, skip_group_check=check)
                nc.tensor.matmul(o, l[0], r[1], start=False, stop=False, skip_group_check=check)
                return nc.tensor.matmul(o, l[1], r[0], start=False, stop=stop, skip_group_check=check)

            def need_slab(base_n, j, it=0, per=0):
                pe.wait_ge(s["slab_split"], it * per + (base_n + j + 3))

            def project(o, b, c0, width, k_tiles, rhs, k0=0, before=None):
                for k in range(k_tiles):
                    c = c0 + k * width
                    if before:
                        before(k)
                    ins = mm3(o, (w_hi[b][:, c:c + P], w_lo[b][:, c:c + P]),
                              (rhs[0][:, k0 + k, :], rhs[1][:, k0 + k, :]), k == 0, k == k_tiles - 1)
                return ins.then_inc(group, 1)

            def stats(o, src, col=None):
                nc.tensor.matmul(o, ones[:], src, start=True, stop=True).then_inc(s["st_ps"], 1)
                if col is not None:
                    columns(col, src)

            def columns(col, src):
                for t in range(TT):
                    ins = nc.tensor.matmul(col[:, t:t + 1], src[:, t * P:(t + 1) * P], ones[:, 0:1],
                                           start=True, stop=True)
                ins.then_inc(s["st_ps"], 1)

            def attend(g):
                for kt in range(TT):
                    for n, part in enumerate((pr_hi, pr_lo)):
                        ins = nc.tensor.matmul(po[:, kt * P:T], vst[:, kt, g, :, :].rearrange("p a c -> p (a c)"),
                                               part[g % 2][:, OFF[kt]:OFF[kt] + WID[kt]],
                                               start=(kt == 0 and n == 0), stop=(kt == TT - 1 and n == 1),
                                               skip_group_check=True)
                return ins

            start_at_one(pe, "z_rdy mz_rdy pv_rdy mpv_rdy")

            pe.wait_ge(s["const_in"], 64)
            for t in range(TT):
                pe.wait_ge(x_landed[t], 16)
                for m in range(KT):
                    ins = nc.tensor.transpose(banks[m][:, t * P:(t + 1) * P],
                                              scf[:, t * D + m * P:t * D + (m + 1) * P], ident[:])
                    if t == TT - 1:
                        ins.then_inc(s["xt_ready"], 1)

            pe.wait_ge(s["const_cast"], 5)
            pe.wait_ge(s["h_lo"], KT)
            pe.wait_ge(s["acc_add"], KT - 1)
            stats(po[:], acc[:], pj[:, 0:TT])
            with pe.Fori(0, 2) as i:
                pe.wait_ge(s["w_exp"], i * HALF + 1)
                for n in range(2):
                    need_slab(N_SB, n, i, SB_SLABS)
                    for t in range(TT):
                        for k in range(4):
                            kk, ts = 4 * n + k, slice(t * P, (t + 1) * P)
                            ins = mm3(banks[t], (h_hi[:, kk, ts], h_lo[:, kk, ts]),
                                      (w_hi[n][:, k * T:(k + 1) * T], w_lo[n][:, k * T:(k + 1) * T]),
                                      kk == 0, kk == KT - 1, check=True)
                        if n == 1 or t == TT - 1:
                            ins.then_inc(group, 1)

                def proj_q(p):
                    j = 2 + 2 * (p // 2)
                    need_slab(N_SB, j, i, SB_SLABS)
                    pe.wait_ge(s["k_t"], i * PAIRS + (p + 1))
                    if p == 0:
                        pe.wait_ge(s["st_var"], 2)
                    project(pj[:], j % 2, P * (p % 2), 256, KT, (h_hi, h_lo))

                def proj_k(p):
                    j = 3 + 2 * (p // 2)
                    need_slab(N_SB, j, i, SB_SLABS)
                    pe.wait_ge(s["q_t"], i * PAIRS + (p + 2))
                    project(pj[:], j % 2, P * (p % 2), 256, KT, (h_hi, h_lo))

                def scores(g):
                    z = z_of(g)
                    r = slice(HD * (g % 2), HD * (g % 2) + HD)
                    if g >= 2:
                        pe.wait_ge(s["w_exp"], i * HALF + g)
                    else:
                        pe.wait_ge(s["v_lo"], i * TT + TT)
                    for j in range(TT):
                        ks, qs = slice(j * P, (j + 1) * P), slice(j * P, T)
                        mm3(z[:, OFF[j]:OFF[j] + WID[j]], (kop[r, 0, 0, ks], kop[r, 0, 1, ks]),
                            (qop[r, 0, 0, qs], qop[r, 0, 1, qs]), j != 3, False, check=True)
                        ins = nc.tensor.matmul(z[:, OFF[j]:OFF[j] + P], ident_b[:], negc_b[:], start=False, stop=True,
                                               skip_group_check=True)
                    ins.then_inc(s["z_rdy"], 1)

                def survive(g):
                    z = z_of(g)
                    pe.wait_ge(s["sp_lo"], i * HALF + (g + 1))
                    for j in range(TT):
                        for kt in range(j, TT):
                            for part in (pr_hi, pr_lo):
                                ins = nc.tensor.matmul(z[:, OFF[j] + P * (kt - j):OFF[j] + WID[j]],
                                                       (tri_r if kt == j else ones_r)[:],
                                                       part[g % 2][:, OFF[kt]:OFF[kt] + WID[kt]], start=False,
                                                       stop=(kt == TT - 1), skip_group_check=True)
                    ins.then_inc(s["surv_rdy"], 1)

                def values(g):
                    pe.wait_ge(s["w_lo"], i * HALF + (g + 2))
                    pe.wait_ge(s["o_add"], i * HALF + (g + 1))
                    attend(g).then_inc(s["pv_rdy"], 1)

                proj_q(0)
                proj_k(0)
                for p in range(PAIRS):
                    a, b = 2 * p, 2 * p + 1
                    pe.wait_ge(s["q_lo"], i * PAIRS + (p + 2))
                    pe.wait_ge(s["k_lo"], i * PAIRS + (p + 2))
                    scores(a)
                    scores(b)
                    if p:
                        values(a - 1)
                    if p < PAIRS - 1:
                        proj_q(p + 1)
                    survive(a)
                    if p < PAIRS - 1:
                        proj_k(p + 1)
                    survive(b)
                    values(a)
                values(HALF - 1)

            def out_project(base_n, split_sem, freed):
                for j in range(4):
                    need_slab(base_n, j)
                    for m in range(2):
                        q = 2 * j + m
                        if q == 0:
                            pe.wait_ge(s[split_sem], 2 * PAIRS + 1)
                        if q >= 4:
                            pe.wait_ge(s[freed], q - 3)
                        project(banks[q % 4], j % 2, P * m, 256, KT, (u_hi, u_lo))

            out_project(N_SBO, "o_lo", "so_x")
            pe.wait_ge(s["rope_pos"], 1)
            nc.tensor.matmul(pj[:], ones[0:1, :], scr[0:1, 0, :], start=True, stop=True).then_inc(s["rope_ps"], 1)

            def mlp(layer, base_n, phase):
                m_s = mlp_s[layer]
                pe.sem_inc(m_s["evac"], 4)
                pe.wait_ge(s["h_lo"], phase * KT)
                pe.wait_ge(s["acc_add"], phase * (KT - 1))
                stats(po[:], acc[:])
                with pe.Fori(0, NFB) as i:
                    for j in range(MLP_SLABS):
                        need_slab(base_n, j, i, MLP_SLABS)
                        for m in range(2):
                            q = 2 * j + m
                            pe.wait_ge(m_s["evac"], i * MLP_GROUPS + (q + 1))
                            if j < 4:
                                project(banks[q % 4], j % 2, P * m, 256, KT, (h_hi, h_lo))
                            else:
                                def split_done(k, q=q):
                                    if q == KT:
                                        pe.wait_ge(m_s["lo"], i * KT + (k + 2))
                                project(banks[q % 4], j % 2, P * m, 256, KT, (u_hi, u_lo), before=split_done)

            mlp(0, N_MLP0, 2)

            pe.wait_ge(s["h_lo"], 3 * KT)
            pe.wait_ge(s["acc_add"], 3 * (KT - 1))
            stats(po[:], acc[:])
            pe.wait_ge(mlp_s[0]["evac"], MLP_GROUPS * NFB + 4)
            need_slab(N_DOWN, 0)
            for m in range(KRT):
                project(banks[m], 0, P * m, 256, KT, (h_hi, h_lo))
            need_slab(N_DOWN, 1)
            project(banks[2], 1, 0, P, KT, (h_hi, h_lo))
            pe.wait_ge(s["gq_lo"], KT)
            need_slab(N_DOWN, 2)
            for m in range(2):
                project(banks[3 + m], 0, P * m, 256, KT, (u_hi, u_lo))
            need_slab(N_DOWN, 3)
            project(banks[5], 1, 0, P, KT, (u_hi, u_lo))
            pe.wait_ge(s["ra_u"], 1)
            nc.tensor.matmul(pj[:], swap[:], scr[:, 4, :], start=True, stop=True).then_inc(s["rb_ps"], 1)
            pe.wait_ge(s["lat_add"], 1)
            pe.wait_ge(s["lat_u"], KRT)
            pe.wait_ge(s["st_var"], 4)
            stats(po[:], tab_a[:], banks[0][:, 0:TT])
            pe.wait_ge(s["lat_add"], 3)
            pe.wait_ge(s["kr_v"], 2)
            stats(pj[:], tab_b[:])

            with pe.Fori(0, 2) as i:
                pe.wait_ge(s["lat_lo"], KRT + QRT)
                pe.wait_ge(s["st_var"], 7)
                pe.wait_ge(s["mw_lo"], i * HALF + 1)
                for kt in range(KRT):
                    need_slab(N_MLA, kt, i, MLA_SLABS)
                    for t in range(TT):
                        ts = slice(t * P, (t + 1) * P)
                        ins = mm3(banks[t], (h_hi[:, kt, ts], h_lo[:, kt, ts]),
                                  (w_hi[kt][:, 0:T], w_lo[kt][:, 0:T]), kt == 0, kt == KRT - 1, check=True)
                        if kt == KRT - 1 or t == TT - 1:
                            ins.then_inc(group, 1)

                def proj_kn(p):
                    j = 2 + p // 2
                    need_slab(N_MLA, j, i, MLA_SLABS)
                    pe.wait_ge(s["mq_t"], i * HALF + (2 * p + 1))
                    project(pj[:], j % 2, 1536 + P * (p % 2), 256, KRT, (h_hi, h_lo))

                def proj_mq(g):
                    if g % 2 == 0:
                        pe.wait_ge(s["mk_t"], i * HALF + (g + 2))
                    else:
                        pe.wait_ge(s["mq_t"], i * HALF + (g + 1))
                    project(pj[:], (g // 4) % 2, P * (g % 4), 4 * P, QRT, (h_hi, h_lo), k0=KRT)

                def mla_scores(g):
                    z = z_of(g)
                    b = g % 2
                    if g < 2:
                        pe.wait_ge(s["mv_lo"], i * TT + TT)
                    else:
                        pe.wait_ge(s["mw_lo"], i * HALF + g)
                    pe.wait_ge(s["mq_lo"], i * HALF + (g + 2))
                    for n in range(TT):
                        t = TT - 1 - n
                        qs = slice(t * P, (t + 1) * P)
                        mm3(z[:, OFF[n]:OFF[n] + WID[n]], (qop[:, b, 0, qs], qop[:, b, 1, qs]),
                            (kop[:, b, 0, 0:WID[n]], kop[:, b, 1, 0:WID[n]]), n != 3, False, check=True)
                        ins = nc.tensor.matmul(z[:, OFF[n] + t * P:OFF[n] + (t + 1) * P], ident_b[:], negm_b[:],
                                               start=False, stop=True, skip_group_check=True)
                    ins.then_inc(s["mz_rdy"], 1)

                def turn(g):
                    z = z_of(g)
                    pe.wait_ge(s["m_norm"], i * HALF + (g + 1))
                    for j in range(TT):
                        for t in range(j, TT):
                            c, o = OFF[TT - 1 - t] + j * P, OFF[j] + P * (t - j)
                            ins = nc.tensor.transpose(z[:, o:o + P], prob[g % 2][:, c:c + P], ident[:])
                    ins.then_inc(s["mt_rdy"], 1)

                def mla_values(g):
                    pe.wait_ge(s["mw_lo"], i * HALF + (g + 2))
                    pe.wait_ge(s["mo_add"], i * HALF + (g + 1))
                    attend(g).then_inc(s["mpv_rdy"], 1)

                proj_kn(0)
                proj_mq(0)
                proj_mq(1)
                for p in range(PAIRS):
                    a, b = 2 * p, 2 * p + 1
                    more = p < PAIRS - 1
                    pe.wait_ge(s["mk_lo"], i * PAIRS + (p + 2))
                    if p == 0:
                        pe.wait_ge(s["kr_lo"], 1)
                    mla_scores(a)
                    mla_scores(b)
                    if more:
                        proj_kn(p + 1)
                    if p:
                        mla_values(a - 1)
                    if more:
                        proj_mq(a + 2)
                    turn(a)
                    if more:
                        proj_mq(b + 2)
                    turn(b)
                    mla_values(a)
                mla_values(HALF - 1)

            out_project(N_MLAO, "mo_lo", "mo_x")
            mlp(1, N_MLP1, 4)

            pe.wait_ge(s["acc_add"], 5 * (KT - 1))
            columns(pj[:, 0:TT], acc[:])
            pe.wait_ge(s["f_xg"], KT)
            for t in range(TT):
                for n in range(2):
                    if t >= 2:
                        pe.wait_ge(s["f_out_s" if n else "f_out_v"], t - 1)
                    for m in range(4):
                        ins = nc.tensor.transpose(banks[2 * (t % 2) + n][:, m * P:(m + 1) * P],
                                                  xT[:, 4 * n + m, t * P:(t + 1) * P], ident[:])
                    ins.then_inc(s["f_tr"], 1)

        @block.scalar
        def _(act):
            start_at_one(act, "w_exp")
            for l in range(2):
                act.sem_inc(mlp_s[l]["sq"], 1)
            with nc.allow_non_contiguous_dma(reason="gains, a word per partition and tile"):
                for src, g in ((attn_norm.rearrange("l (t p) -> p l t", p=P), G_ATTN),
                               (mlp_norm.rearrange("l (t p) -> p l t", p=P), G_MLP),
                               (kv_norm.rearrange("(a t p) -> p a t", p=P, a=1), G_KV),
                               (final_norm.rearrange("(a t p) -> p a t", p=P, a=1), G_FIN),
                               (kv_lat.rearrange("(a t p) -> p a t", p=P, a=1), G_LKV),
                               (q_lat.rearrange("a (t p) -> p a t", p=P), G_LQ)):
                    a, t = src.shape[1], src.shape[2]
                    for l in range(a):
                        act.dma_start(gain[:, g + l * t:g + (l + 1) * t], src[:, l, :]).then_inc(s["gain_in"], 16)
            act.wait_ge(s["gain_in"], 16 * 8)

            def square(m, phase):
                if m >= 3:
                    act.wait_ge(s["acc_add"], phase * (KT - 1) + m - 2)
                dst = acc if m == 0 else sq_tmp[m % 2]
                nc.scalar.activation(dst[:], xT[:, m, :], ACT.Square).then_inc(s["sq_done"], 1)

            def prepare(m, phase, g):
                nc.scalar.activation(h_hi[:, m, :], xT[:, m, :], ACT.Copy, scale=gcol(g + m)).then_inc(s["h_hi"], 1)
                square(m, phase)

            def slab_hi(b, landed, used, parts):
                act.wait_ge(raw_landed[b], landed)
                act.wait_ge(group, used)
                for to, frm in parts:
                    nc.scalar.activation(to(w_hi[b]), frm(raw[b]), ACT.Copy).then_inc(s["slab_hi_act"], 1)

            def mlp_slab_hi(n_in, g0, i, j):
                slab_hi(j % 2, i * (16 * MLP_SLABS) + (16 * n_in + 32 * (j // 2 + 1)),
                        i * MLP_GROUPS + (g0 + 2 * (j - 1)), full(SLAB))

            def root(n, dst):
                act.wait_ge(s["st_var"], n)
                nc.scalar.activation(dst, dst, ACT.Sqrt).then_inc(s["st_sqrt"], 1)

            for m in range(KT):
                act.wait_ge(s["x_done"], m + 1)
                prepare(m, 0, G_ATTN)
            root(1, r_tok[:])
            root(2, r_col[:])

            def store_values(i, g0, per, hi_sem):
                for t in range(TT):
                    act.wait_ge(group, i * per + (g0 + 2 + t))
                    nc.scalar.activation(vst[:, t, :, 0, :], banks[t].rearrange("p (h c) -> p h c", c=HD), ACT.Copy,
                                         scale=r_col[:, t:t + 1]).then_inc(s[hi_sem], 1)

            def half_out(i, g, sems, tmp):
                pv, o_tmp, o_add = sems
                act.wait_ge(s[pv], i * HALF + (g + 2))
                if g >= 2:
                    act.wait_ge(s[o_add], i * HALF + g)
                else:
                    act.wait_ge(s[o_add], i * HALF + 1)
                nc.scalar.activation(tmp(g), po[HD:P, :], ACT.Copy).then_inc(s[o_tmp], 1)

            def pair_hi(i, p, o_add, o_hi):
                act.wait_ge(s[o_add], i * HALF + (2 * p + 3))
                nc.scalar.activation(u_hi[:, i * PAIRS + p, :], t_out, ACT.Copy).then_inc(s[o_hi], 1)

            act.wait_ge(s["st_inv"], 2)
            nc.scalar.preload_act_table_set("natural_log_exp_and_others")
            with act.Fori(0, 2) as i:
                store_values(i, G_SB, SB_GROUPS, "v_hi")
                sb_tmp = (lambda g: t_half[HD * (g % 2):HD * (g % 2) + HD, :])
                sb_sems = ("pv_rdy", "o_tmp", "o_add")

                def operand_hi(p, which):
                    act.wait_ge(s[which + "_t"], i * PAIRS + (p + 2))
                    act.wait_ge(s["z_rdy"], i * HALF + (2 * p + 1))
                    op = qop if which == "q" else kop
                    nc.scalar.activation(op[:, 0, 0, :], t_proj, ACT.Copy).then_inc(s[which + "_hi"], 1)

                def exp_abs(g):
                    act.wait_ge(s["z_rdy"], i * HALF + (g + 2))
                    act.wait_ge(s["w_lo"], i * HALF + max(g, 1))
                    nc.scalar.activation(prob[g % 2], z_of(g), ACT.Abs).then_inc(s["z_abs"], 1)
                    act.wait_ge(s["z_abs"], i * HALF + (g + 1))
                    nc.scalar.activation(prob[g % 2], prob[g % 2], ACT.Exp, scale=-1.0).then_inc(s["sp_exp"], 1)

                def log_one(g):
                    act.wait_ge(s["sp_exp"], i * HALF + (g + 1))
                    nc.scalar.activation(prob[g % 2], prob[g % 2], ACT.Ln, bias=1.0).then_inc(s["sp_ln"], 1)

                def weights(g):
                    act.wait_ge(s["surv_rdy"], i * HALF + (g + 1))
                    nc.scalar.activation(prob[g % 2], z_of(g), ACT.Exp).then_inc(s["w_exp"], 1)
                    act.wait_ge(s["w_exp"], i * HALF + (g + 2))
                    nc.scalar.activation(pr_hi[g % 2][:], prob[g % 2], ACT.Copy).then_inc(s["w_hi"], 1)

                operand_hi(0, "q")
                operand_hi(0, "k")
                for p in range(PAIRS):
                    a, b = 2 * p, 2 * p + 1
                    exp_abs(a)
                    log_one(a)
                    exp_abs(b)
                    log_one(b)
                    if p:
                        half_out(i, a - 1, sb_sems, sb_tmp)
                        pair_hi(i, p - 1, "o_add", "o_hi")
                    if p < PAIRS - 1:
                        operand_hi(p + 1, "q")
                    weights(a)
                    if p < PAIRS - 1:
                        operand_hi(p + 1, "k")
                    weights(b)
                    half_out(i, a, sb_sems, sb_tmp)
                half_out(i, HALF - 1, sb_sems, sb_tmp)
                pair_hi(i, PAIRS - 1, "o_add", "o_hi")

            def after_out(x_sem, phase, g, n_in, g0):
                for m in range(KT):
                    act.wait_ge(s[x_sem], m + 1)
                    prepare(m, phase, g)
                    if m in (1, 3):
                        slab_hi(m // 2, 16 * n_in + 64, g0 + m + 1, full(SLAB))
                    elif m in (5, 7):
                        mlp_slab_hi(n_in + 4, g0 + KT, 0, (m - 5) // 2)

            act.wait_ge(s["o_lo"], 2 * PAIRS + 1)
            act.dma_start(scr[0:1, 3, :].bitcast(I32), pos_in).then_inc(s["pos_landed"], 16)
            after_out("so_x", 1, G_MLP, N_SBO, G_SBO)

            for steps_done, tab in ((8, sin_t), (16, cos_t)):
                act.wait_ge(s["rope_v"], steps_done)
                nc.scalar.activation(tab, tab, ACT.Sin).then_inc(s["rope_s"], 1)

            def mlp(layer, n_stat, n_in, g0, tail):
                m_s = mlp_s[layer]
                root(n_stat, r_tok[:])

                def hidden(i, q):
                    act.wait_ge(m_s["evac"], i * MLP_GROUPS + (4 + q + 1))
                    act.wait_ge(m_s["lo"], i * KT + max(q, 1))
                    nc.scalar.activation(scr[:, 6 + q % 2, :], scr[:, 4 + q % 2, :], ACT.Square).then_inc(m_s["sq"], 1)
                    act.wait_ge(m_s["sq"], i * KT + (q + 2))
                    nc.scalar.activation(u_hi[:, q, :], scr[:, 6 + q % 2, :], ACT.Copy).then_inc(m_s["hi"], 1)

                def first(i):
                    for q in range(KT):
                        hidden(i, q)
                        if q % 2:
                            mlp_slab_hi(n_in, g0, i, 2 + q // 2)

                with act.Fori(0, NFB - 1) as i:
                    first(i)
                    for j in range(6, 10):
                        mlp_slab_hi(n_in, g0, i, j)
                first(NFB - 1)
                for m in range(KT):
                    act.wait_ge(m_s["evac"], (NFB - 1) * MLP_GROUPS + 4 + KT + m + 1)
                    tail(m)
                    if m in (1, 3):
                        mlp_slab_hi(n_in, g0, NFB - 1, 6 + m // 2)

            def to_down(m):
                prepare(m, 2, G_KV)
                if m == 5:
                    slab_hi(0, 16 * N_DOWN + 32, G_DOWN - 2, full(SLAB))
                if m == 7:
                    slab_hi(1, 16 * N_DOWN + 32, G_DOWN, rope_parts)

            mlp(0, 3, N_MLP0, G_MLP0, to_down)
            for m in range(KT):
                nc.scalar.activation(u_hi[:, m, :], xT[:, m, :], ACT.Copy, scale=gcol(G_ATTN + KT + m))\
                    .then_inc(s["gq_hi"], 1)
            slab_hi(0, 16 * N_DOWN + 64, G_DOWN + KRT, full(SLAB))
            slab_hi(1, 16 * N_DOWN + 64, G_DOWN + KRT + 1, full(KT * P))
            root(4, r_tok[:])
            act.wait_ge(s["st_ps"], 4)
            for n in range(KRT + QRT):
                act.wait_ge(s["lat_u"], n + 1)
                if n == 3:
                    act.wait_ge(s["lat_add"], 1)
                if n == 4:
                    act.wait_ge(s["lat_add"], 2)
                dst = (tab_a, acc, tab_b, acc, acc)[n]
                src = scr[:, (2, 3, 5, 6, 7)[n], :]
                nc.scalar.activation(dst[:], src, ACT.Square).then_inc(s["lat_sq"], 1)
                act.wait_ge(group, G_DOWN + KRT + 1)
                nc.scalar.activation(h_hi[:, n, :], src, ACT.Copy, scale=gcol(G_LKV + n)).then_inc(s["lat_hi"], 1)
            act.wait_ge(s["kr_v"], 3)
            for b in range(2):
                nc.scalar.activation(kop[HD:P, b, 0, :], scr[HD:P, 4, :], ACT.Copy).then_inc(s["kr_hi"], 1)
            root(5, acc[:])
            root(6, r_col[:])
            root(7, tab_b[:])

            act.wait_ge(s["st_inv"], 7)
            with act.Fori(0, 2) as i:
                store_values(i, G_MLA, MLA_GROUPS, "mv_hi")
                mla_tmp = (lambda g: scr[HD:P, 5 + g % 2, :])
                mla_sems = ("mpv_rdy", "mo_tmp", "mo_add")

                def key_hi(p):
                    act.wait_ge(s["mk_t"], i * HALF + (2 * p + 2))
                    act.wait_ge(s["mz_rdy"], i * HALF + (2 * p + 1))
                    nc.scalar.activation(kop[0:HD, :, 0, :], scr[0:HD, 5:7, :], ACT.Copy).then_inc(s["mk_hi"], 1)

                def query_hi(g):
                    act.wait_ge(s["mq_t"], i * HALF + (g + 2))
                    act.wait_ge(s["mz_rdy"], i * HALF + max(g, 1))
                    nc.scalar.activation(qop[:, g % 2, 0, :], r_tok[:], ACT.Copy).then_inc(s["mq_hi"], 1)

                def soft(g):
                    z, b = z_of(g), g % 2
                    act.wait_ge(s["m_max"], i * HALF + (g + 1))
                    for n in range(TT):
                        c = slice(OFF[n], OFF[n] + WID[n])
                        nc.scalar.activation(prob[b][:, c], z[:, c], ACT.Exp, bias=nmax[:, b, n:n + 1],
                                             accum_out=rsum[:, b, n:n + 1]).then_inc(s["m_exp"], 1)

                def weight_hi(g):
                    act.wait_ge(s["mt_rdy"], i * HALF + (g + 1))
                    act.wait_ge(s["mpv_rdy"], i * HALF + max(g, 1))
                    nc.scalar.activation(pr_hi[g % 2][:], z_of(g), ACT.Copy).then_inc(s["mw_hi"], 1)

                key_hi(0)
                query_hi(0)
                query_hi(1)
                for p in range(PAIRS):
                    a, b = 2 * p, 2 * p + 1
                    more = p < PAIRS - 1
                    soft(a)
                    soft(b)
                    if more:
                        key_hi(p + 1)
                    if p:
                        half_out(i, a - 1, mla_sems, mla_tmp)
                        pair_hi(i, p - 1, "mo_add", "mo_hi")
                    if more:
                        query_hi(a + 2)
                    weight_hi(a)
                    if more:
                        query_hi(b + 2)
                    weight_hi(b)
                    half_out(i, a, mla_sems, mla_tmp)
                half_out(i, HALF - 1, mla_sems, mla_tmp)
                pair_hi(i, PAIRS - 1, "mo_add", "mo_hi")

            after_out("mo_x", 3, G_MLP + KT, IN_MLAO, G_MLAO)

            def last_tail(m):
                square(m, 4)
                act.wait_ge(s["sq_done"], 4 * KT + m + 1)
                nc.scalar.activation(xT[:, m, :], xT[:, m, :], ACT.Copy, scale=gcol(G_FIN + m)).then_inc(s["f_xg"], 1)

            mlp(1, 8, IN_MLP1, G_MLP1, last_tail)
            root(9, r_col[:])
            act.wait_ge(s["st_inv"], 9)
            for t in range(TT):
                act.wait_ge(s["f_tr"], 2 * t + 2)
                nc.scalar.activation(scf[:, t * D + T:(t + 1) * D], banks[2 * (t % 2) + 1], ACT.Copy,
                                     scale=r_col[:, t:t + 1]).then_inc(s["f_out_s"], 1)

        @block.vector
        def _(dve):
            v = nc.vector
            start_at_one(dve, "q_t k_t q_lo k_lo w_lo o_add o_lo mk_lo mq_t mq_lo mw_lo mo_add mo_lo")
            for l in range(2):
                dve.sem_inc(mlp_s[l]["lo"], 1)

            def lower(m, phase, g):
                dve.wait_ge(s["h_hi"], phase * KT + m + 1)
                v.scalar_tensor_tensor(h_lo[:, m, :], xT[:, m, :], gcol(g + m), h_hi[:, m, :].bitcast(F32),
                                       ALU.mult, ALU.subtract).then_inc(s["h_lo"], 1)
                add_square(m, phase)

            def add_square(m, phase):
                if m:
                    dve.wait_ge(s["sq_done"], phase * KT + m + 1)
                    dve.wait_ge(s["acc_add"], phase * (KT - 1) + m - 1)
                    v.tensor_tensor(acc[:], acc[:], sq_tmp[m % 2][:], ALU.add).then_inc(s["acc_add"], 1)

            def mean(n, dst, src, width):
                dve.wait_ge(s["st_ps"], n)
                v.tensor_scalar(dst, src, 1.0 / width, EPS, ALU.mult, ALU.add).then_inc(s["st_var"], 1)

            def inverse(n, dst):
                dve.wait_ge(s["st_sqrt"], n)
                v.reciprocal(dst, dst).then_inc(s["st_inv"], 1)

            dve.wait_ge(s["gain_in"], 16 * 8)
            for m in range(KT):
                dve.wait_ge(s["xt_ready"], m + 1)
                v.tensor_copy(xT[:, m, :], banks[m]).then_inc(s["x_done"], 1)
                if m:
                    lower(m - 1, 0, G_ATTN)
            lower(KT - 1, 0, G_ATTN)
            dve.wait_ge(s["const_cast"], 5)
            mean(1, r_tok[:], po[:], D)
            mean(2, r_col[:], pj[:, 0:TT], D)
            inverse(1, r_tok[:])
            inverse(2, r_col[:])
            dve.wait_ge(s["st_inv"], 2)
            v.tensor_scalar(tab_a[:], r_tok[:], SB_SCALE, None, ALU.mult).then_inc(s["q_scale"], 1)
            dve.wait_ge(s["q_scale"], 1)

            def value_lo(i, hi_sem, lo_sem):
                for t in range(TT):
                    dve.wait_ge(s[hi_sem], i * TT + (t + 1))
                    v.scalar_tensor_tensor(vst[:, t, :, 1, :], banks[t].rearrange("p (h c) -> p h c", c=HD),
                                           r_col[:, t:t + 1], vst[:, t, :, 0, :].bitcast(F32), ALU.mult,
                                           ALU.subtract).then_inc(s[lo_sem], 1)

            def add_out(i, g, sems, tmp):
                o_tmp, o_add, o_lo = sems
                dve.wait_ge(s[o_tmp], i * HALF + (g + 1))
                dve.wait_ge(s[o_lo], i * PAIRS + (g // 2 + 1))
                r = slice(HD * (g % 2), HD * (g % 2) + HD)
                v.tensor_tensor(t_out[r, :], po[0:HD, :], tmp(g), ALU.add).then_inc(s[o_add], 1)

            def pair_lo(i, p, o_hi, o_lo, o_add):
                dve.wait_ge(s[o_hi], i * PAIRS + (p + 1))
                v.tensor_tensor(u_lo[:, i * PAIRS + p, :], t_out, u_hi[:, i * PAIRS + p, :].bitcast(F32),
                                ALU.subtract).then_inc(s[o_lo], 1)

            with dve.Fori(0, 2) as i:
                value_lo(i, "v_hi", "v_lo")
                sb_tmp = (lambda g: t_half[HD * (g % 2):HD * (g % 2) + HD, :])
                sb_sems = ("o_tmp", "o_add", "o_lo")

                def scale(p, which):
                    dve.wait_ge(group, i * SB_GROUPS + (G_SB + sb_group(which, p)))
                    if which == "q":
                        dve.wait_ge(s["k_lo"], i * PAIRS + (p + 1))
                    else:
                        dve.wait_ge(s["q_lo"], i * PAIRS + (p + 2))
                    v.tensor_tensor(t_proj, pj[:], (tab_a if which == "q" else r_tok)[:], ALU.mult)\
                        .then_inc(s[which + "_t"], 1)

                def operand_lo(p, which):
                    op = qop if which == "q" else kop
                    dve.wait_ge(s[which + "_hi"], i * PAIRS + (p + 1))
                    v.tensor_tensor(op[:, 0, 1, :], t_proj, op[:, 0, 0, :].bitcast(F32), ALU.subtract)\
                        .then_inc(s[which + "_lo"], 1)

                def softplus(g):
                    dve.wait_ge(s["sp_ln"], i * HALF + (g + 1))
                    v.scalar_tensor_tensor(prob[g % 2], z_of(g), 0.0, prob[g % 2], ALU.max, ALU.add)\
                        .then_inc(s["sp_sum"], 1)

                def split_plus(g):
                    dve.wait_ge(s["sp_sum"], i * HALF + (g + 1))
                    dve.wait_ge(s["pv_rdy"], i * HALF + max(g, 1))
                    v.tensor_copy(pr_hi[g % 2][:], prob[g % 2]).then_inc(s["sp_hi"], 1)
                    dve.wait_ge(s["sp_hi"], i * HALF + (g + 1))
                    v.tensor_tensor(pr_lo[g % 2][:], prob[g % 2], pr_hi[g % 2][:].bitcast(F32), ALU.subtract)\
                        .then_inc(s["sp_lo"], 1)

                def weight_lo(g):
                    dve.wait_ge(s["w_hi"], i * HALF + (g + 1))
                    v.tensor_tensor(pr_lo[g % 2][:], prob[g % 2], pr_hi[g % 2][:].bitcast(F32), ALU.subtract)\
                        .then_inc(s["w_lo"], 1)

                scale(0, "q")
                operand_lo(0, "q")
                scale(0, "k")
                operand_lo(0, "k")
                for p in range(PAIRS):
                    a, b = 2 * p, 2 * p + 1
                    more = p < PAIRS - 1
                    softplus(a)
                    split_plus(a)
                    if more:
                        scale(p + 1, "q")
                    softplus(b)
                    split_plus(b)
                    if p:
                        add_out(i, a - 1, sb_sems, sb_tmp)
                        pair_lo(i, p - 1, "o_hi", "o_lo", "o_add")
                    if more:
                        operand_lo(p + 1, "q")
                    weight_lo(a)
                    if more:
                        scale(p + 1, "k")
                        operand_lo(p + 1, "k")
                    weight_lo(b)
                    add_out(i, a, sb_sems, sb_tmp)
                add_out(i, HALF - 1, sb_sems, sb_tmp)
                pair_lo(i, PAIRS - 1, "o_hi", "o_lo", "o_add")

            def add_x(m, bank, count, sem):
                dve.wait_ge(group, count)
                v.tensor_tensor(xT[:, m, :], bank, xT[:, m, :], ALU.add).then_inc(sem, 1)

            def after_out(g0, x_sem, phase, g):
                for m in range(KT):
                    add_x(m, banks[m % 4], g0 + m + 1, s[x_sem])
                    if m:
                        lower(m - 1, phase, g)
                lower(KT - 1, phase, g)

            after_out(G_SBO, "so_x", 1, G_MLP)

            steps = [0]

            def step(ins):
                steps[0] += 1
                ins.then_inc(s["rope_v"], 1)
                dve.wait_ge(s["rope_v"], steps[0])

            dve.wait_ge(s["pos_landed"], 16)
            v.tensor_copy(scr[0:1, 0, :], scr[0:1, 3, :].bitcast(I32)).then_inc(s["rope_pos"], 1)
            ang, turns = scr[:, 2, :], scr[:, 3, :]
            dve.wait_ge(s["rope_ps"], 1)
            step(v.tensor_scalar(ang, pj[:], cols[:, COL_FREQ:COL_FREQ + 1], None, ALU.mult))
            for tab, quarter in ((sin_t, 0.0), (cos_t, 0.25)):
                step(v.tensor_scalar(turns, ang, 1.0 / TWO_PI, quarter, ALU.mult, ALU.add))
                step(v.tensor_scalar(turns, turns, ROUNDER, None, ALU.add))
                step(v.tensor_scalar(turns, turns, ROUNDER, None, ALU.subtract))
                step(v.scalar_tensor_tensor(tab, turns, -PI_A, ang, ALU.mult, ALU.add))
                step(v.scalar_tensor_tensor(tab, turns, -PI_B, tab, ALU.mult, ALU.add))
                step(v.scalar_tensor_tensor(tab, turns, -PI_C, tab, ALU.mult, ALU.add))
                if quarter:
                    step(v.tensor_scalar(tab, tab, TWO_PI * quarter, None, ALU.add))
                step(v.tensor_scalar(tab, tab, PI_SAFE, -PI_SAFE, ALU.min, ALU.max))

            def mlp(layer, g0, n_stat, tail):
                m_s = mlp_s[layer]
                mean(n_stat, r_tok[:], po[:], D)
                inverse(n_stat, r_tok[:])
                dve.wait_ge(s["st_inv"], n_stat)

                def relu(i, q):
                    dve.wait_ge(group, i * MLP_GROUPS + (g0 + q + 1))
                    dve.wait_ge(m_s["sq"], i * KT + max(q, 1))
                    v.scalar_tensor_tensor(scr[:, 4 + q % 2, :], banks[q % 4], 0.0, r_tok[:], ALU.max, ALU.mult)\
                        .then_inc(m_s["evac"], 1)

                def hidden_lo(i, q):
                    dve.wait_ge(m_s["hi"], i * KT + (q + 1))
                    v.tensor_tensor(u_lo[:, q, :], scr[:, 6 + q % 2, :], u_hi[:, q, :].bitcast(F32), ALU.subtract)\
                        .then_inc(m_s["lo"], 1)

                def first(i):
                    for q in range(KT):
                        relu(i, q)
                        if q:
                            hidden_lo(i, q - 1)
                    hidden_lo(i, KT - 1)

                with dve.Fori(0, NFB - 1) as i:
                    first(i)
                    for m in range(KT):
                        add_x(m, banks[m % 4], i * MLP_GROUPS + (g0 + KT + m + 1), m_s["evac"])
                first(NFB - 1)
                for m in range(KT):
                    add_x(m, banks[m % 4], (NFB - 1) * MLP_GROUPS + g0 + KT + m + 1, m_s["evac"])
                    if m:
                        tail(m - 1)
                tail(KT - 1)

            mlp(0, G_MLP0, 3, lambda m: lower(m, 2, G_KV))
            for m in range(KT):
                dve.wait_ge(s["gq_hi"], m + 1)
                v.scalar_tensor_tensor(u_lo[:, m, :], xT[:, m, :], gcol(G_ATTN + KT + m), u_hi[:, m, :].bitcast(F32),
                                       ALU.mult, ALU.subtract).then_inc(s["gq_lo"], 1)
            mean(4, r_tok[:], po[:], D)
            inverse(4, r_tok[:])
            dve.wait_ge(s["st_inv"], 4)

            lat_tile = (2, 3, 5, 6, 7)
            lat_bank = (0, 1, 3, 4, 5)

            def latent(n):
                dve.wait_ge(group, G_DOWN + lat_bank[n] + 1)
                v.tensor_tensor(scr[:, lat_tile[n], :], banks[lat_bank[n]], r_tok[:], ALU.mult)\
                    .then_inc(s["lat_u"], 1)

            def latent_lo(n):
                dve.wait_ge(s["lat_hi"], n + 1)
                v.scalar_tensor_tensor(h_lo[:, n, :], scr[:, lat_tile[n], :], gcol(G_LKV + n),
                                       h_hi[:, n, :].bitcast(F32), ALU.mult, ALU.subtract).then_inc(s["lat_lo"], 1)

            def latent_add(n, dst, count):
                dve.wait_ge(s["lat_sq"], n + 1)
                dve.wait_ge(s["lat_add"], count)
                v.tensor_tensor(dst[:], dst[:], acc[:], ALU.add).then_inc(s["lat_add"], 1)

            latent(0)
            latent(1)
            latent_add(1, tab_a, 0)
            dve.wait_ge(group, G_DOWN + KRT + 1)
            v.tensor_tensor(scr[:, 4, :], banks[2], r_tok[:], ALU.mult).then_inc(s["ra_u"], 1)
            latent_lo(0)
            latent_lo(1)
            for n in range(2, 5):
                latent(n)
                if n > 2:
                    latent_add(n, tab_b, n - 2)
                latent_lo(n)
            dve.wait_ge(s["rope_s"], 2)
            dve.wait_ge(s["rb_ps"], 1)
            v.tensor_tensor(scr[:, 4, :], scr[:, 4, :], cos_t, ALU.mult).then_inc(s["kr_v"], 1)
            v.tensor_tensor(r_tok[:], pj[:], sin_t, ALU.mult).then_inc(s["kr_v"], 1)
            dve.wait_ge(s["kr_v"], 2)
            v.tensor_tensor(scr[:, 4, :], scr[:, 4, :], r_tok[:], ALU.add).then_inc(s["kr_v"], 1)
            for b in range(2):
                dve.wait_ge(s["kr_hi"], b + 1)
                ins = v.tensor_tensor(kop[HD:P, b, 1, :], scr[HD:P, 4, :], kop[HD:P, b, 0, :].bitcast(F32),
                                      ALU.subtract)
            ins.then_inc(s["kr_lo"], 1)
            mean(5, acc[:], po[:], KR)
            mean(6, r_col[:], banks[0][:, 0:TT], KR)
            mean(7, tab_b[:], pj[:], QR)
            inverse(5, acc[:])
            inverse(6, r_col[:])
            inverse(7, tab_b[:])
            v.tensor_scalar(tab_a[:], cos_t, cols[:, COL_COS:COL_COS + 1], cols[:, COL_ONE:COL_ONE + 1],
                            ALU.mult, ALU.add).then_inc(s["tab_v"], 1)
            dve.wait_ge(s["tab_v"], 1)
            v.scalar_tensor_tensor(tab_a[:], sin_t, cols[:, COL_SIN:COL_SIN + 1], tab_a[:], ALU.mult, ALU.add)\
                .then_inc(s["tab_v"], 1)
            dve.wait_ge(s["tab_v"], 2)
            dve.wait_ge(s["st_inv"], 7)
            v.tensor_tensor(tab_a[:], tab_a[:], tab_b[:], ALU.mult).then_inc(s["tab_v"], 1)
            dve.wait_ge(s["tab_v"], 3)

            with dve.Fori(0, 2) as i:
                value_lo(i, "mv_hi", "mv_lo")
                mla_tmp = (lambda g: scr[HD:P, 5 + g % 2, :])
                mla_sems = ("mo_tmp", "mo_add", "mo_lo")

                def key(p):
                    dve.wait_ge(group, i * MLA_GROUPS + (G_MLA + mla_group("k", p)))
                    dve.wait_ge(s["mk_lo"], i * PAIRS + (p + 1))
                    for b in range(2):
                        r = slice(HD * b, HD * b + HD)
                        v.tensor_tensor(scr[0:HD, 5 + b, :], pj[r, :], acc[r, :], ALU.mult).then_inc(s["mk_t"], 1)

                def key_lo(p):
                    dve.wait_ge(s["mk_hi"], i * PAIRS + (p + 1))
                    v.tensor_tensor(kop[0:HD, :, 1, :], scr[0:HD, 5:7, :], kop[0:HD, :, 0, :].bitcast(F32),
                                    ALU.subtract).then_inc(s["mk_lo"], 1)

                def query(g):
                    dve.wait_ge(group, i * MLA_GROUPS + (G_MLA + mla_group("q", g)))
                    dve.wait_ge(s["mq_lo"], i * HALF + (g + 1))
                    v.tensor_tensor(r_tok[:], pj[:], tab_a[:], ALU.mult).then_inc(s["mq_t"], 1)

                def query_lo(g):
                    dve.wait_ge(s["mq_hi"], i * HALF + (g + 1))
                    v.tensor_tensor(qop[:, g % 2, 1, :], r_tok[:], qop[:, g % 2, 0, :].bitcast(F32), ALU.subtract)\
                        .then_inc(s["mq_lo"], 1)

                def row_max(g):
                    dve.wait_ge(s["mz_rdy"], i * HALF + (g + 2))
                    z = z_of(g)
                    for n in range(TT):
                        ins = v.tensor_reduce(nmax[:, g % 2, n:n + 1], z[:, OFF[n]:OFF[n] + WID[n]], AX.X, ALU.max,
                                              negate=True)
                    ins.then_inc(s["m_max"], 1)

                inv_count = [0]

                def normalise(g):
                    b = g % 2
                    dve.wait_ge(s["m_exp"], i * (HALF * TT) + TT * (g + 1))
                    v.reciprocal(rsum[:, b, :], rsum[:, b, :]).then_inc(s["tab_v"], 1)
                    dve.wait_ge(s["tab_v"], i * HALF + (4 + g))
                    for n in range(TT):
                        c = slice(OFF[n], OFF[n] + WID[n])
                        ins = v.tensor_scalar(prob[b][:, c], prob[b][:, c], rsum[:, b, n:n + 1], None, ALU.mult)
                    ins.then_inc(s["m_norm"], 1)

                def weight_lo(g):
                    dve.wait_ge(s["mw_hi"], i * HALF + (g + 1))
                    v.tensor_tensor(pr_lo[g % 2][:], z_of(g), pr_hi[g % 2][:].bitcast(F32), ALU.subtract)\
                        .then_inc(s["mw_lo"], 1)

                key(0)
                key_lo(0)
                query(0)
                query_lo(0)
                query(1)
                query_lo(1)
                for p in range(PAIRS):
                    a, b = 2 * p, 2 * p + 1
                    more = p < PAIRS - 1
                    row_max(a)
                    row_max(b)
                    if more:
                        key(p + 1)
                        key_lo(p + 1)
                    if p:
                        add_out(i, a - 1, mla_sems, mla_tmp)
                        pair_lo(i, p - 1, "mo_hi", "mo_lo", "mo_add")
                    normalise(a)
                    if more:
                        query(a + 2)
                    normalise(b)
                    if more:
                        query_lo(a + 2)
                    weight_lo(a)
                    if more:
                        query(b + 2)
                        query_lo(b + 2)
                    weight_lo(b)
                    add_out(i, a, mla_sems, mla_tmp)
                add_out(i, HALF - 1, mla_sems, mla_tmp)
                pair_lo(i, PAIRS - 1, "mo_hi", "mo_lo", "mo_add")

            after_out(G_MLAO, "mo_x", 3, G_MLP + KT)
            mlp(1, G_MLP1, 8, lambda m: add_square(m, 4))
            mean(9, r_col[:], pj[:, 0:TT], D)
            inverse(9, r_col[:])
            dve.wait_ge(s["st_inv"], 9)
            for t in range(TT):
                dve.wait_ge(s["f_tr"], 2 * t + 1)
                v.tensor_scalar(scf[:, t * D:t * D + T], banks[2 * (t % 2)], r_col[:, t:t + 1], None, ALU.mult)\
                    .then_inc(s["f_out_v"], 1)


_INS = ["x", "positions", "attn_norm", "mlp_norm", "sb_w_qkv", "sb_w_o", "kv_norm", "mla_w_dkv", "mla_kv_lat_norm",
        "mla_w_ukv", "mla_w_dq", "mla_q_lat_norm", "mla_w_uq", "mla_w_o", "mlp_w1", "mlp_w2", "final_norm"]


def kernel(**inputs):
    import numpy as _np
    import concourse.bacc as _bacc
    from concourse import mybir as _mybir
    from concourse.bass_utils import run_bass_kernel_spmd as _run

    nc = _bacc.Bacc("TRN2", target_bir_lowering=False, num_devices=1)
    arrays, args = {}, []
    for name in _INS:
        a = _np.ascontiguousarray(inputs[name])
        arrays[f"in_{name}_dram"] = a
        args.append(nc.dram_tensor(f"in_{name}_dram", a.shape, _mybir.dt.from_np(a.dtype), kind="ExternalInput").ap())
    c = constants()
    arrays["in_consts_dram"] = c
    args.append(nc.dram_tensor("in_consts_dram", c.shape, _mybir.dt.float32, kind="ExternalInput").ap())
    args.append(nc.dram_tensor("out_0_dram", (1, T, D), _mybir.dt.float32, kind="ExternalOutput").ap())
    build(nc, *args)
    r = _run(nc, [arrays], core_ids=[0])
    return r.results[0]["out_0_dram"]
```

```python
from contextlib import ExitStack

import numpy as np

import concourse.bass as bass
from concourse import mybir

F32 = mybir.dt.float32
F32R = mybir.dt.float32r
BF16 = mybir.dt.bfloat16
I32 = mybir.dt.int32
ACT = mybir.ActivationFunctionType
ALU = mybir.AluOpType
AX = mybir.AxisListType

P = 128
D = 1024
T = 512
KT = D // P
TT = T // P
FF = 4096
FB = 1024
NFB = FF // FB
HD = 64
HALF = 8
PAIRS = HALF // 2
ROPE = 32
NOPE = 64
QH = NOPE + ROPE
QR = 384
KR = 256
QRT = QR // P
KRT = KR // P
EPS = 1e-6
SB_SCALE = HD ** -0.5
MLA_SCALE = QH ** -0.5
SLAB = 2048
MASKED = -1e30

OFF = (0, 512, 1024, 896)
WID = tuple(T - P * j for j in range(TT))
PACK = sum(WID)
BLOCKS = (0, 1, 3, 2)
PARTS = (slice(0, T), slice(T, PACK))
PH = len(PARTS) * HALF

TWO_PI = 6.283185307179586
PI_A = 6.28125
PI_B = float(np.float32(np.float32(TWO_PI - PI_A).view(np.uint32).__and__(np.uint32(0xFFFFF000)).view(np.float32)))
PI_C = TWO_PI - PI_A - PI_B
ROUNDER = 1.5 * 2.0 ** 23
PI_SAFE = 3.1415925

C_IDENT, C_SWAP, C_TRI, C_ONES, C_NEGC, C_NEGM = range(6)
COL_FREQ, COL_COS, COL_SIN, COL_ONE = range(4)
G_ATTN, G_MLP, G_KV, G_FIN, G_LKV, G_LQ, G_END = 0, 16, 32, 40, 48, 50, 53

N_SB = 0
SB_SLABS = 6
N_SBO = N_SB + 2 * SB_SLABS
N_MLP0 = N_SBO + 4
MLP_SLABS = 8
N_DOWN = N_MLP0 + NFB * MLP_SLABS
N_MLA = N_DOWN + 4
MLA_SLABS = 4
N_MLAO = N_MLA + 2 * MLA_SLABS
N_MLP1 = N_MLAO + 4


def constants():
    c = np.zeros((P, 6 * P + 4), np.float32)
    k, q = np.arange(P)[:, None], np.arange(P)[None, :]
    m = [c[:, n * P:(n + 1) * P] for n in range(6)]
    m[C_IDENT][:] = k == q
    half = ROPE // 2
    m[C_SWAP][:] = 1.0 * ((q % ROPE >= half) & (k == q - half)) - 1.0 * ((q % ROPE < half) & (k == q + half))
    m[C_TRI][:] = -1.0 * (k >= q)
    m[C_ONES][:] = -1.0
    m[C_NEGC][:] = MASKED * (k >= q)
    m[C_NEGM][:] = MASKED * (k // 64 < q // 64)
    col = c[:, 6 * P:]
    freq = np.float32(10000.0) ** (-np.arange(0, ROPE, 2, dtype=np.float32) / np.float32(ROPE))
    row = np.arange(P)
    col[:, COL_FREQ] = freq[row % half]
    col[:, COL_COS] = MLA_SCALE * ((row >= 64) & (row < 96))
    col[:, COL_SIN] = MLA_SCALE * (1.0 * (row >= 112) - 1.0 * ((row >= 96) & (row < 112)))
    col[:, COL_ONE] = MLA_SCALE * (row < 64)
    return c


SB_GROUPS = 1 + TT + 2 * PAIRS
MLP_GROUPS = 4 * KT // 2
MLA_GROUPS = TT + 3 * PAIRS
G_SB = 2
G_SBO = G_SB + 2 * SB_GROUPS
G_MLP0 = G_SBO + KT
G_DOWN = G_MLP0 + NFB * MLP_GROUPS
G_MLA = G_DOWN + KRT + 1 + QRT
G_MLAO = G_MLA + 2 * MLA_GROUPS
G_MLP1 = G_MLAO + KT


def sb_group(kind, n=0):
    return {"v_first": 1, "v": 2 + n, "q": TT + 2 + 2 * n, "k": TT + 3 + 2 * n}[kind]


def mla_group(kind, n=0):
    return {"v": 1 + n, "k": TT + 1 + 3 * n, "q": TT + 2 + 3 * (n // 2) + n % 2}[kind]


def build(nc, x_in, pos_in, attn_norm, mlp_norm, w_qkv, w_o, kv_norm, w_dkv, kv_lat, w_ukv, w_dq, q_lat, w_uq,
          mla_wo, w1, w2, final_norm, consts, out):
    with ExitStack() as ctx:
        def sb(name, shape, dt):
            return ctx.enter_context(nc.sbuf_tensor(name, shape, dt))

        names = """ident_in const_in gain0_in gain_in pos_landed const_cast
            slab_asked slab_begun slab_hi slab_hi_act slab_split group
            xt_ready x_done r_var r_sqrt r_inv diag r_row h_hi h_lo sum_sq sq_done acc_add gq_hi gq_lo
            st_ps st_var st_sqrt st_inv q_scale
            v_hi v_lo z_rdy z_abs sp_exp sp_ln sp_sum sp_hi sp_lo surv_rdy w_exp w_hi w_lo pv_rdy
            o_tmp o_add o_hi o_lo q_t q_hi q_lo k_t k_hi k_lo so_x
            rope_pos rope_ps rope_v rope_s
            lat_u lat_sq lat_add lat_hi lat_lo ra_u rb_ps kr_v kr_hi kr_lo tab_v
            mv_hi mv_lo mz_rdy m_max m_exp m_inv m_norm m_norm_b mt_rdy mw_hi mw_lo mpv_rdy mo_tmp mo_add mo_hi mo_lo
            mq_t mq_hi mq_lo mk_t mk_hi mk_lo mo_x
            f_xg f_tr f_out_v f_out_s out_done""".split()
        s = {n: ctx.enter_context(nc.semaphore(n)) for n in names}
        x_landed = [ctx.enter_context(nc.semaphore(f"x_landed{t}")) for t in range(TT)]
        raw_landed = [ctx.enter_context(nc.semaphore(f"raw_landed{b}")) for b in range(2)]
        mlp_s = [{n: ctx.enter_context(nc.semaphore(f"mlp{l}_{n}")) for n in "evac sq hi lo".split()}
                 for l in range(2)]
        group = s["group"]

        xT = sb("xT", [P, KT, T], F32)
        h_hi, h_lo = sb("h_hi", [P, KT, T], F32R), sb("h_lo", [P, KT, T], F32R)
        u_hi, u_lo = sb("u_hi", [P, KT, T], F32R), sb("u_lo", [P, KT, T], F32R)
        raw = [sb(f"raw{b}", [P, SLAB], F32) for b in range(2)]
        w_hi = [sb(f"w_hi{b}", [P, SLAB], F32R) for b in range(2)]
        w_lo = [sb(f"w_lo{b}", [P, SLAB], F32R) for b in range(2)]
        vst = sb("vst", [P, TT, HALF, 2, HD], F32R)
        qop = sb("qop", [P, 2, 2, T], F32R)
        kop = sb("kop", [P, 2, 2, T], F32R)
        pr_hi = [sb(f"pr_hi{b}", [P, PACK], F32R) for b in range(2)]
        pr_lo = [sb(f"pr_lo{b}", [P, PACK], F32R) for b in range(2)]
        scr = sb("scr", [P, 8, T], F32)
        r_tok = sb("r_tok", [P, T], F32)
        tab_a = sb("tab_a", [P, T], F32)
        tab_b = sb("tab_b", [P, T], F32)
        acc = sb("acc", [P, T], F32)
        ident = sb("ident", [P, P], F32)
        swap = sb("swap", [P, P], F32)
        ones = sb("ones", [P, P], F32)
        tri_r, ones_r = sb("tri_r", [P, P], F32R), sb("ones_r", [P, P], F32R)
        ident_b, negc_b, negm_b = (sb(n, [P, P], BF16) for n in ("ident_b", "negc_b", "negm_b"))
        cols = sb("cols", [P, 4], F32)
        gain = sb("gain", [P, G_END], F32)
        r_col = sb("r_col", [P, TT], F32)
        nmax = sb("nmax", [P, 2, TT], F32)
        rsum = sb("rsum", [P, 2, TT], F32)

        zb = ctx.enter_context(nc.psum_tensor("zb", [P, 6, T], F32))
        pj = ctx.enter_context(nc.psum_tensor("pj", [P, T], F32))
        po = ctx.enter_context(nc.psum_tensor("po", [P, T], F32))
        zf = zb[:].rearrange("p b t -> p (b t)")
        banks = [zb[:, b, :] for b in range(6)] + [pj[:], po[:]]

        scf = scr[:].rearrange("p a t -> p (a t)")
        prob = [scf[:, b * PACK:(b + 1) * PACK] for b in range(2)]
        t_proj, t_half, t_out = scr[:, 5, :], scr[:, 6, :], scr[:, 7, :]
        sq_tmp = [tab_a, tab_b]
        spare_sq = u_lo[:, 0:2, :].rearrange("p a t -> p (a t)")
        cos_t, sin_t = scr[:, 0, :], scr[:, 1, :]

        def z_of(g):
            return zf[:, (g % 2) * 3 * T:(g % 2) * 3 * T + PACK]

        def out_bank(n, t):
            return banks[(4, 5, 7, 0, 1, 2, 3, 4)[n * TT + t]]

        def gcol(n):
            return gain[:, n:n + 1]

        def start_at_one(engine, which):
            for n in which.split():
                engine.sem_inc(s[n], 1)

        block = ctx.enter_context(nc.Block())

        @block.sync
        def _(sp):
            sp.dma_start(ident[:], consts[:, C_IDENT * P:(C_IDENT + 1) * P]).then_inc(s["ident_in"], 16)
            for t in range(TT):
                sp.dma_start(scf[:, t * D:(t + 1) * D], x_in[0, t * P:(t + 1) * P, :]).then_inc(x_landed[t], 16)

            def slab(base_n, j, puts, it=0, per=0):
                sp.wait_ge(s["slab_split"], it * per + (base_n + j + 1))
                sp.sem_inc(s["slab_asked"], 1)
                for dst, src in puts:
                    sp.dma_start(dst(raw[j % 2]), src).then_inc(raw_landed[j % 2], 16)

            def tiles(src, r0, rows, c0, width):
                kt = rows // P // 2
                return [(lambda r, n=n: r[:, 0:2 * kt * width].rearrange("p (k c) -> p k c", c=width)[
                            :, n * kt:(n + 1) * kt, :],
                         src[bass.ds(r0 + n * kt * P, kt * P), bass.ds(c0, width)].rearrange(
                             "(k p) c -> p k c", p=P)) for n in range(2)]

            wq = w_qkv[0]
            with sp.Fori(0, 2) as i:
                for n in range(2):
                    slab(N_SB, n, tiles(wq, n * T, T, i * T + 2 * D, T), i, SB_SLABS)
                for quad in range(2):
                    for which in range(2):
                        slab(N_SB, 2 + 2 * quad + which, tiles(wq, 0, D, i * T + (quad * 256 + which * D), 256),
                             i, SB_SLABS)
            for j in range(4):
                slab(N_SBO, j, tiles(w_o[0], 0, D, 256 * j, 256))

            def mlp(layer, base_n):
                with sp.Fori(0, NFB) as i:
                    for j in range(4):
                        slab(base_n, j, tiles(w1[layer], 0, D, i * FB + 256 * j, 256), i, MLP_SLABS)
                    for j in range(4):
                        slab(base_n, 4 + j, tiles(w2[layer], i * FB, FB, 256 * j, 256), i, MLP_SLABS)

            mlp(0, N_MLP0)
            slab(N_DOWN, 0, tiles(w_dkv, 0, D, 0, KR))
            slab(N_DOWN, 1, tiles(w_dkv, 0, D, KR, ROPE))
            slab(N_DOWN, 2, tiles(w_dq[0], 0, D, 0, 256))
            slab(N_DOWN, 3, tiles(w_dq[0], 0, D, 256, P))
            ukv = w_ukv.rearrange("(k p) (h c) -> k p h c", p=P, c=P)
            uq = w_uq[0].rearrange("(k p) (h c) -> k p h c", p=P, c=QH)
            with sp.Fori(0, 2) as i:
                def values_in(kt):
                    return (lambda r: r[:, T * kt:T * (kt + 1)].rearrange("p (h c) -> p h c", c=HD),
                            ukv[kt, :, bass.ds(i * HALF, HALF), HD:P])

                def keys_in(kt, quad, at):
                    return (lambda r: r[:, at + 256 * kt:at + 256 * (kt + 1)].rearrange("p (h c) -> p h c", c=HD),
                            ukv[kt, :, bass.ds(i * HALF + 4 * quad, 4), 0:HD])

                def queries_in(kt, h0, heads, at):
                    w = heads * QH
                    return (lambda r: r[:, at + w * kt:at + w * (kt + 1)].rearrange("p (h c) -> p h c", c=QH),
                            uq[kt, :, bass.ds(i * HALF + h0, heads), :])

                for j, puts in enumerate((
                        [values_in(kt) for kt in range(KRT)] + [keys_in(kt, 0, 1024) for kt in range(KRT)],
                        [queries_in(kt, 0, 4, 0) for kt in range(QRT)],
                        [keys_in(kt, 1, 0) for kt in range(KRT)] + [queries_in(kt, 4, 2, 512) for kt in range(QRT)],
                        [queries_in(kt, 6, 2, 0) for kt in range(QRT)])):
                    slab(N_MLA, j, puts, i, MLA_SLABS)
            for j in range(4):
                slab(N_MLAO, j, tiles(mla_wo[0], 0, D, 256 * j, 256))
            mlp(1, N_MLP1)
            for t in range(TT):
                sp.wait_ge(s["f_out_v"], t + 1)
                sp.wait_ge(s["f_out_s"], t + 1)
                sp.dma_start(out[0, t * P:(t + 1) * P, :], scf[:, t * D:(t + 1) * D]).then_inc(s["out_done"], 16)
            sp.wait_ge(s["out_done"], 16 * TT)

        IN_MLA = N_MLA
        IN_MLA_J = (2 * KRT, QRT, 3 * KRT + QRT, 2 * QRT)
        IN_MLAO = tuple(IN_MLA + 2 * n for n in IN_MLA_J[2:])
        IN_MLP1 = tuple(n + 4 for n in IN_MLAO)
        HI_OUT0 = 2 + 2 * 2
        HI_MLP0 = HI_OUT0 + 2
        HI_DOWN = HI_MLP0 + NFB * MLP_SLABS
        HI_OUT1 = HI_DOWN + 3 + 4
        HI_MLP1 = HI_OUT1 + 2

        def full(width):
            return [(lambda w: w[:, 0:width], lambda w: w[:, 0:width])]

        rope_parts = [((lambda w, r=r: w[:, 0:KT * P].rearrange("p (k r c) -> p k r c", k=KT, r=4)[:, :, r, :]),
                       (lambda w: w[:, 0:KT * ROPE].rearrange("p (k c) -> p k c", k=KT))) for r in range(4)]

        @block.gpsimd
        def _(gp):
            gp.dma_start(swap[:], consts[:, C_SWAP * P:(C_SWAP + 1) * P]).then_inc(s["const_in"], 16)
            gp.dma_start(r_tok[:], consts[:, C_TRI * P:(C_NEGM + 1) * P]).then_inc(s["const_in"], 16)
            gp.dma_start(cols[:], consts[:, 6 * P:6 * P + 4]).then_inc(s["const_in"], 16)
            gp.sem_inc(s["slab_split"], 1)
            gp.sem_inc(group, 2)
            gp.memset(ones[:], 1.0).then_inc(s["const_cast"], 1)
            gp.wait_ge(s["const_in"], 48)
            gp.tensor_copy(tri_r[:], r_tok[:, 0:P]).then_inc(s["slab_split"], 1)
            gp.tensor_copy(ones_r[:], r_tok[:, P:2 * P]).then_inc(s["const_cast"], 1)
            gp.tensor_copy(negc_b[:], r_tok[:, 2 * P:3 * P]).then_inc(s["const_cast"], 1)
            gp.tensor_copy(negm_b[:], r_tok[:, 3 * P:4 * P]).then_inc(s["const_cast"], 1)
            gp.wait_ge(s["ident_in"], 16)
            gp.tensor_copy(ident_b[:], ident[:]).then_inc(s["const_cast"], 1)

            def split(b, landed, used, seen, parts):
                gp.wait_ge(raw_landed[b], landed)
                gp.wait_ge(group, used)
                gp.sem_inc(s["slab_begun"], 1)
                for to, frm in parts:
                    gp.tensor_copy(to(w_hi[b]), frm(raw[b])).then_inc(s["slab_hi"], 1)
                gp.wait_ge(s["slab_hi"], seen + len(parts))
                for to, frm in parts:
                    ins = gp.tensor_tensor(to(w_lo[b]), frm(raw[b]), to(w_hi[b]).bitcast(F32), ALU.subtract)
                ins.then_inc(s["slab_split"], 1)

            def split_lo(b, seen, parts):
                gp.wait_ge(s["slab_hi_act"], seen)
                for to, frm in parts:
                    ins = gp.tensor_tensor(to(w_lo[b]), frm(raw[b]), to(w_hi[b]).bitcast(F32), ALU.subtract)
                ins.then_inc(s["slab_split"], 1)

            last = [sb_group("v_first"), sb_group("v", TT - 1), sb_group("q", 1), sb_group("k", 1),
                    sb_group("q", 3), sb_group("k", 3)]
            for j in range(2):
                split_lo(j, j + 1, full(SLAB))
            with gp.Fori(0, 2) as i:
                for j in range(2, 2 + SB_SLABS):
                    if j < 4:
                        split_lo(j % 2, i * 2 + (j + 1), full(SLAB))
                    else:
                        split(j % 2, i * (16 * SB_SLABS) + 32 * (j // 2 + 1), i * SB_GROUPS + (G_SB + last[j - 2]),
                              i * (SB_SLABS - 2) + (j - 4), full(SLAB))

            def last_out_slabs(hi0):
                for j in range(2):
                    split_lo(j, hi0 + j + 1, full(SLAB))

            def mlp_slabs(hi0):
                with gp.Fori(0, NFB) as i:
                    for j in range(MLP_SLABS):
                        split_lo(j % 2, i * MLP_SLABS + (hi0 + j + 1), full(SLAB))

            last_out_slabs(HI_OUT0)
            mlp_slabs(HI_MLP0)
            for j, (done, parts) in enumerate(((1, full(SLAB)), (5, rope_parts), (6, full(SLAB)), (7, full(KT * P)))):
                split_lo(j % 2, HI_DOWN + done, parts)

            def head_cols(c0, c1, width, heads, at):
                n = QRT * heads * width
                return lambda w: w[:, at:at + n].rearrange("p (k h c) -> p k h c", k=QRT, h=heads)[:, :, :, c0:c1]

            def query_parts(heads, at):
                half = ROPE // 2
                return [(head_cols(a, b, P, heads, at), head_cols(c, d, QH, heads, at)) for a, b, c, d in
                        ((0, QH, 0, QH), (QH, QH + half, NOPE + half, QH), (QH + half, P, NOPE, NOPE + half))]

            seen = 2 * (SB_SLABS - 2)
            mla_parts = (full(2 * T + 512), query_parts(4, 0), full(512) + query_parts(2, 512), query_parts(2, 0))
            per_it = sum(len(parts) for parts in mla_parts)
            used = (-1, 0, mla_group("k", 1), mla_group("q", 3))
            with gp.Fori(0, 2) as i:
                for j, parts in enumerate(mla_parts):
                    split(j % 2, i * (16 * IN_MLA_J[2 + j % 2]) + 16 * (IN_MLA + IN_MLA_J[j]),
                          i * MLA_GROUPS + (G_MLA + used[j]),
                          i * per_it + (seen + sum(len(m) for m in mla_parts[:j])), parts)
            seen += 2 * per_it
            for j in range(2):
                split(j, 16 * IN_MLAO[j] + 32, G_MLAO - 1 + j, seen + j, full(SLAB))
            last_out_slabs(HI_OUT1)
            mlp_slabs(HI_MLP1)

        @block.tensor
        def _(pe):
            def mm3(o, l, r, start, stop, check=False):
                nc.tensor.matmul(o, l[0], r[0], start=start, stop=False, skip_group_check=check)
                nc.tensor.matmul(o, l[0], r[1], start=False, stop=False, skip_group_check=check)
                return nc.tensor.matmul(o, l[1], r[0], start=False, stop=stop, skip_group_check=check)

            def need_slab(base_n, j, it=0, per=0):
                pe.wait_ge(s["slab_split"], it * per + (base_n + j + 3))

            def project(o, b, c0, width, k_tiles, rhs, k0=0, before=None):
                for k in range(k_tiles):
                    c = c0 + k * width
                    if before:
                        before(k)
                    ins = mm3(o, (w_hi[b][:, c:c + P], w_lo[b][:, c:c + P]),
                              (rhs[0][:, k0 + k, :], rhs[1][:, k0 + k, :]), k == 0, k == k_tiles - 1)
                return ins.then_inc(group, 1)

            def stats(o, src, col=None):
                nc.tensor.matmul(o, ones[:], src, start=True, stop=True).then_inc(s["st_ps"], 1)
                if col is not None:
                    columns(col, src)

            def columns(col, src):
                for t in range(TT):
                    ins = nc.tensor.matmul(col[:, t:t + 1], src[:, t * P:(t + 1) * P], ones[:, 0:1],
                                           start=True, stop=True)
                ins.then_inc(s["st_ps"], 1)

            def attend(i, g, split_sem):
                for kt in range(TT):
                    if kt < 2:
                        pe.wait_ge(split_sem, i * PH + (2 * g + kt + 2))
                    for n, part in enumerate((pr_hi, pr_lo)):
                        ins = nc.tensor.matmul(po[:, kt * P:T], vst[:, kt, g, :, :].rearrange("p a c -> p (a c)"),
                                               part[g % 2][:, OFF[kt]:OFF[kt] + WID[kt]],
                                               start=(kt == 0 and n == 0), stop=(kt == TT - 1 and n == 1),
                                               skip_group_check=True)
                return ins

            start_at_one(pe, "z_rdy mz_rdy pv_rdy mpv_rdy")

            pe.wait_ge(s["ident_in"], 16)
            for t in range(TT):
                pe.wait_ge(x_landed[t], 16)
                for m in range(KT):
                    ins = nc.tensor.transpose(banks[m][:, t * P:(t + 1) * P],
                                              scf[:, t * D + m * P:t * D + (m + 1) * P], ident[:])
                    if t == TT - 1:
                        ins.then_inc(s["xt_ready"], 1)

            pe.wait_ge(s["const_cast"], 5)
            pe.wait_ge(s["x_done"], KT)
            pe.wait_ge(s["diag"], TT)
            nc.tensor.matmul(po[:], ones[:], acc[:], start=True, stop=True).then_inc(s["r_row"], 1)
            with pe.Fori(0, 2) as i:
                pe.wait_ge(s["w_exp"], i * PH + 1)
                for n in range(2):
                    need_slab(N_SB, n, i, SB_SLABS)
                    order = [(k, t) for k in range(4) for t in range(TT)]
                    for k, t in order if n == 0 else sorted(order, key=lambda kt: kt[1]):
                        kk, ts = 4 * n + k, slice(t * P, (t + 1) * P)
                        if t == 0:
                            pe.wait_ge(s["h_lo"], kk + 1)
                        ins = mm3(banks[t], (h_hi[:, kk, ts], h_lo[:, kk, ts]),
                                  (w_hi[n][:, k * T:(k + 1) * T], w_lo[n][:, k * T:(k + 1) * T]),
                                  kk == 0, kk == KT - 1, check=True)
                        if k == 3 and (n == 1 or t == TT - 1):
                            ins.then_inc(group, 1)

                def proj_q(p):
                    j = 2 + 2 * (p // 2)
                    need_slab(N_SB, j, i, SB_SLABS)
                    pe.wait_ge(s["k_t"], i * PAIRS + (p + 1))
                    project(pj[:], j % 2, P * (p % 2), 256, KT, (h_hi, h_lo))

                def proj_k(p):
                    j = 3 + 2 * (p // 2)
                    need_slab(N_SB, j, i, SB_SLABS)
                    if p == 0:
                        pe.wait_ge(s["o_add"], i * HALF + 1)
                        pe.wait_ge(s["q_scale"], 1)
                    else:
                        pe.wait_ge(s["q_t"], i * PAIRS + (p + 2))
                    project(po[:] if p == 0 else pj[:], j % 2, P * (p % 2), 256, KT, (h_hi, h_lo))

                def scores(g):
                    z = z_of(g)
                    r = slice(HD * (g % 2), HD * (g % 2) + HD)
                    if g >= 2:
                        pe.wait_ge(s["w_exp"], i * PH + (2 * g - 1))
                    else:
                        pe.wait_ge(s["v_lo"], i * TT + TT)
                    for j in range(TT):
                        ks, qs = slice(j * P, (j + 1) * P), slice(j * P, T)
                        mm3(z[:, OFF[j]:OFF[j] + WID[j]], (kop[r, 0, 0, ks], kop[r, 0, 1, ks]),
                            (qop[r, 0, 0, qs], qop[r, 0, 1, qs]), j != 3, False, check=True)
                        ins = nc.tensor.matmul(z[:, OFF[j]:OFF[j] + P], ident_b[:], negc_b[:], start=False, stop=True,
                                               skip_group_check=True)
                    ins.then_inc(s["z_rdy"], 1)

                def survive(g):
                    z = z_of(g)
                    pe.wait_ge(s["sp_lo"], i * PH + 2 * (g + 1))
                    for j in range(TT):
                        for kt in range(j, TT):
                            for part in (pr_hi, pr_lo):
                                ins = nc.tensor.matmul(z[:, OFF[j] + P * (kt - j):OFF[j] + WID[j]],
                                                       (tri_r if kt == j else ones_r)[:],
                                                       part[g % 2][:, OFF[kt]:OFF[kt] + WID[kt]], start=False,
                                                       stop=(kt == TT - 1), skip_group_check=True)
                    ins.then_inc(s["surv_rdy"], 1)

                def values(g):
                    pe.wait_ge(s["o_add"], i * HALF + (g + 1))
                    attend(i, g, s["w_lo"]).then_inc(s["pv_rdy"], 1)

                proj_q(0)
                proj_k(0)
                for p in range(PAIRS):
                    a, b = 2 * p, 2 * p + 1
                    pe.wait_ge(s["q_lo"], i * PAIRS + (p + 2))
                    pe.wait_ge(s["k_lo"], i * PAIRS + (p + 2))
                    scores(a)
                    scores(b)
                    if p:
                        values(a - 1)
                    if p < PAIRS - 1:
                        proj_q(p + 1)
                    survive(a)
                    if p < PAIRS - 1:
                        proj_k(p + 1)
                    survive(b)
                    values(a)
                values(HALF - 1)

            def out_project(base_n, split_sem, freed, halfway):
                for j in range(4):
                    need_slab(base_n, j)
                    for m in range(2):
                        q = 2 * j + m
                        if q >= 4:
                            pe.wait_ge(s[freed], q - 3)

                        def pair_split(k, q=q):
                            if q == 0:
                                pe.wait_ge(s[split_sem], k + 2)
                        project(banks[q % 4], j % 2, P * m, 256, KT, (u_hi, u_lo), before=pair_split)
                    if j == 1:
                        halfway()

            def spread_positions():
                pe.wait_ge(s["rope_pos"], 1)
                nc.tensor.matmul(pj[:], ones[0:1, :], scr[0:1, 0, :], start=True, stop=True)\
                    .then_inc(s["rope_ps"], 1)

            out_project(N_SBO, "o_lo", "so_x", spread_positions)

            def mlp(layer, base_n, phase):
                m_s = mlp_s[layer]
                pe.sem_inc(m_s["evac"], 4)

                def block_of(i, first=False):
                    for j in range(MLP_SLABS):
                        need_slab(base_n, j, i, MLP_SLABS)
                        for m in range(2):
                            q = 2 * j + m
                            pe.wait_ge(m_s["evac"], i * MLP_GROUPS + (q + 1))

                            def split_done(k, q=q):
                                if q == KT:
                                    pe.wait_ge(m_s["lo"], i * KT + (k + 2))
                                if q == 0 and first:
                                    pe.wait_ge(s["h_lo"], (phase - 1) * KT + k + 1)
                            project(banks[q % 4], j % 2, P * m, 256, KT, (h_hi, h_lo) if j < 4 else (u_hi, u_lo),
                                    before=split_done)
                            if q == 0 and first:
                                pe.wait_ge(s["acc_add"], (phase - 1) * (KT - 1))
                                stats(po[:], acc[:])

                block_of(0, first=True)
                with pe.Fori(1, NFB) as i:
                    block_of(i)

            mlp(0, N_MLP0, 2)

            need_slab(N_DOWN, 0)
            for m in range(KRT):
                pe.wait_ge(mlp_s[0]["evac"], MLP_GROUPS * NFB + m + 1)
                project(banks[m], 0, P * m, 256, KT, (h_hi, h_lo),
                        before=lambda k: pe.wait_ge(s["h_lo"], 2 * KT + k + 1))
                if m == 0:
                    pe.wait_ge(s["acc_add"], 2 * (KT - 1))
                    stats(po[:], acc[:])
            pe.wait_ge(mlp_s[0]["evac"], MLP_GROUPS * NFB + 4)
            need_slab(N_DOWN, 1)
            project(banks[2], 1, 0, P, KT, (h_hi, h_lo))
            pe.wait_ge(s["gq_lo"], KT)
            need_slab(N_DOWN, 2)
            project(banks[3], 0, 0, 256, KT, (u_hi, u_lo))
            project(banks[4], 0, P, 256, KT, (u_hi, u_lo))
            pe.wait_ge(s["ra_u"], 1)
            nc.tensor.matmul(pj[:], swap[:], scr[:, 4, :], start=True, stop=True).then_inc(s["rb_ps"], 1)
            pe.wait_ge(s["lat_add"], 1)
            pe.wait_ge(s["lat_u"], KRT)
            pe.wait_ge(s["st_var"], 2)
            stats(po[:], tab_a[:], banks[0][:, 0:TT])
            need_slab(N_DOWN, 3)
            project(banks[5], 1, 0, P, KT, (u_hi, u_lo))
            pe.wait_ge(s["lat_add"], 3)
            pe.wait_ge(s["kr_v"], 2)
            stats(pj[:], tab_b[:])

            with pe.Fori(0, 2) as i:
                pe.wait_ge(s["lat_lo"], KRT)
                pe.wait_ge(s["st_var"], 4)
                pe.wait_ge(s["mw_lo"], i * PH + 1)
                need_slab(N_MLA, 0, i, MLA_SLABS)
                for t in range(TT):
                    ts = slice(t * P, (t + 1) * P)
                    for kt in range(KRT):
                        c = slice(kt * T, (kt + 1) * T)
                        ins = mm3(banks[t], (h_hi[:, kt, ts], h_lo[:, kt, ts]), (w_hi[0][:, c], w_lo[0][:, c]),
                                  kt == 0, kt == KRT - 1)
                    ins.then_inc(group, 1)

                def proj_kn(p):
                    need_slab(N_MLA, 2 * (p // 2), i, MLA_SLABS)
                    pe.wait_ge(s["mq_t"], i * HALF + (2 * p + 1))
                    if p == 0:
                        pe.wait_ge(s["st_var"], 5)
                    project(pj[:], 0, (0 if p // 2 else 2 * T) + P * (p % 2), 256, KRT, (h_hi, h_lo))

                def proj_mq(g):
                    if g == 0:
                        pe.wait_ge(s["lat_lo"], KRT + QRT)
                    if g == 0:
                        pe.wait_ge(s["mo_add"], i * HALF + 1)
                    elif g == 1 or g % 2 == 0:
                        pe.wait_ge(s["mk_t"], i * HALF + (g // 2 * 2 + 2))
                    else:
                        pe.wait_ge(s["mq_t"], i * HALF + (g + 1))
                    j, c0, heads = ((1, P * g, 4), (2, 512 + P * (g - 4), 2), (3, P * (g - 6), 2))[max(g // 2 - 1, 0)]
                    need_slab(N_MLA, j, i, MLA_SLABS)
                    project(po[:] if g == 0 else pj[:], j % 2, c0, heads * P, QRT, (h_hi, h_lo), k0=KRT)

                def mla_scores(g):
                    z = z_of(g)
                    b = g % 2
                    if g < 2:
                        pe.wait_ge(s["mv_lo"], i * TT + TT)
                    else:
                        pe.wait_ge(s["mw_lo"], i * PH + (2 * g - 1))
                    pe.wait_ge(s["mq_lo"], i * HALF + (g + 2))
                    for n in range(TT):
                        t = TT - 1 - n
                        qs = slice(t * P, (t + 1) * P)
                        mm3(z[:, OFF[n]:OFF[n] + WID[n]], (qop[:, b, 0, qs], qop[:, b, 1, qs]),
                            (kop[:, b, 0, 0:WID[n]], kop[:, b, 1, 0:WID[n]]), n != 3, False, check=True)
                        ins = nc.tensor.matmul(z[:, OFF[n] + t * P:OFF[n] + (t + 1) * P], ident_b[:], negm_b[:],
                                               start=False, stop=True, skip_group_check=True)
                    ins.then_inc(s["mz_rdy"], 1)

                def turn(g):
                    z = z_of(g)
                    for n in range(TT):
                        pe.wait_ge(s["m_norm_b" if g % 2 else "m_norm"],
                                   i * (PAIRS * TT) + (TT * (g // 2) + n + 1))
                        t = TT - 1 - n
                        for j in range(t + 1):
                            c, o = OFF[n] + j * P, OFF[j] + P * (t - j)
                            ins = nc.tensor.transpose(z[:, o:o + P], prob[g % 2][:, c:c + P], ident[:])
                    ins.then_inc(s["mt_rdy"], 1)

                def mla_values(g):
                    pe.wait_ge(s["mo_add"], i * HALF + (g + 1))
                    attend(i, g, s["mw_lo"]).then_inc(s["mpv_rdy"], 1)

                proj_kn(0)
                proj_mq(0)
                proj_mq(1)
                for p in range(PAIRS):
                    a, b = 2 * p, 2 * p + 1
                    more = p < PAIRS - 1
                    pe.wait_ge(s["mk_lo"], i * PAIRS + (p + 2))
                    if p == 0:
                        pe.wait_ge(s["kr_lo"], 1)
                    mla_scores(a)
                    mla_scores(b)
                    if more:
                        proj_kn(p + 1)
                    if p:
                        mla_values(a - 1)
                    if more:
                        proj_mq(a + 2)
                    turn(a)
                    turn(b)
                    if more:
                        proj_mq(b + 2)
                    mla_values(a)
                mla_values(HALF - 1)

            out_project(N_MLAO, "mo_lo", "mo_x", lambda: None)
            mlp(1, N_MLP1, 4)

            def to_tokens(n, t):
                for m in range(4):
                    ins = nc.tensor.transpose(out_bank(n, t)[:, m * P:(m + 1) * P],
                                              xT[:, 4 * n + m, t * P:(t + 1) * P], ident[:])
                ins.then_inc(s["f_tr"], 1)

            pe.wait_ge(s["f_xg"], 5)
            for t in range(TT):
                to_tokens(0, t)
            pe.wait_ge(s["acc_add"], 4 * (KT - 1))
            columns(pj[:, 0:TT], acc[:])
            pe.wait_ge(s["f_xg"], KT)
            for t in range(TT):
                if t == TT - 1:
                    pe.wait_ge(s["f_out_v"], 1)
                to_tokens(1, t)

        @block.scalar
        def _(act):
            start_at_one(act, "w_exp")
            for l in range(2):
                act.sem_inc(mlp_s[l]["sq"], 1)

            def load_gain(src, g, sem):
                with nc.allow_non_contiguous_dma(reason="gains, a word per partition and tile"):
                    act.dma_start(gain[:, g:g + src.shape[1]], src).then_inc(sem, 16)

            by_layer = [n.rearrange("l (t p) -> p l t", p=P) for n in (attn_norm, mlp_norm)]
            load_gain(by_layer[0][:, 0, :], G_ATTN, s["gain0_in"])
            for t in range(TT):
                act.wait_ge(x_landed[t], 16)
                nc.scalar.activation(spare_sq, scf[:, t * D:(t + 1) * D], ACT.Square,
                                     accum_out=r_col[:, t:t + 1]).then_inc(s["sum_sq"], 1)
                if t < TT - 1:
                    act.wait_ge(s["sum_sq"], t + 1)

            def square(m, phase):
                if m >= 3:
                    act.wait_ge(s["acc_add"], (phase - 1) * (KT - 1) + m - 2)
                dst = acc if m == 0 else sq_tmp[m % 2]
                nc.scalar.activation(dst[:], xT[:, m, :], ACT.Square).then_inc(s["sq_done"], 1)

            def prepare(m, phase, g):
                nc.scalar.activation(h_hi[:, m, :], xT[:, m, :], ACT.Copy, scale=gcol(g + m)).then_inc(s["h_hi"], 1)
                square(m, phase)

            def slab_hi(b, landed, used, parts):
                act.wait_ge(raw_landed[b], landed)
                act.wait_ge(group, used)
                for to, frm in parts:
                    nc.scalar.activation(to(w_hi[b]), frm(raw[b]), ACT.Copy).then_inc(s["slab_hi_act"], 1)

            def mlp_slab_hi(n_in, g0, i, j):
                slab_hi(j % 2, i * (16 * MLP_SLABS) + (16 * n_in[j % 2] + 32 * (j // 2 + 1)),
                        i * MLP_GROUPS + (g0 + 2 * (j - 1)), full(SLAB))

            def root(n, dst):
                act.wait_ge(s["st_var"], n)
                nc.scalar.activation(dst, dst, ACT.Sqrt).then_inc(s["st_sqrt"], 1)

            act.wait_ge(s["gain0_in"], 16)
            for m in range(KT):
                act.wait_ge(s["x_done"], m + 1)
                nc.scalar.activation(h_hi[:, m, :], xT[:, m, :], ACT.Copy, scale=gcol(G_ATTN + m))\
                    .then_inc(s["h_hi"], 1)
                if m in (1, 5):
                    act.wait_ge(raw_landed[m // 4], 32)
                    nc.scalar.activation(w_hi[m // 4][:], raw[m // 4][:], ACT.Copy).then_inc(s["slab_hi_act"], 1)
                if m == 1:
                    act.wait_ge(s["r_var"], 1)
                    nc.scalar.activation(r_col[:], r_col[:], ACT.Sqrt).then_inc(s["r_sqrt"], 1)
            for src, g in ((by_layer[0][:, 1, :], G_ATTN + KT), (by_layer[1][:, 0, :], G_MLP),
                           (by_layer[1][:, 1, :], G_MLP + KT), (kv_norm.rearrange("(t p) -> p t", p=P), G_KV),
                           (final_norm.rearrange("(t p) -> p t", p=P), G_FIN),
                           (kv_lat.rearrange("(t p) -> p t", p=P), G_LKV),
                           (q_lat.rearrange("a (t p) -> p (a t)", p=P), G_LQ)):
                load_gain(src, g, s["gain_in"])

            def store_value(i, t, done, per, hi_sem):
                act.wait_ge(group, i * per + (done + t))
                nc.scalar.activation(vst[:, t, :, 0, :], banks[t].rearrange("p (h c) -> p h c", c=HD), ACT.Copy,
                                     scale=r_col[:, t:t + 1]).then_inc(s[hi_sem], 1)

            def half_out(i, g, sems, tmp):
                pv, o_tmp, o_add = sems
                act.wait_ge(s[pv], i * HALF + (g + 2))
                if g >= 2:
                    act.wait_ge(s[o_add], i * HALF + g)
                else:
                    act.wait_ge(s[o_add], i * HALF + 1)
                nc.scalar.activation(tmp(g), po[HD:P, :], ACT.Copy).then_inc(s[o_tmp], 1)

            def pair_hi(i, p, o_add, o_hi):
                act.wait_ge(s[o_add], i * HALF + (2 * p + 3))
                nc.scalar.activation(u_hi[:, i * PAIRS + p, :], t_out, ACT.Copy).then_inc(s[o_hi], 1)

            act.wait_ge(s["r_inv"], 1)
            nc.scalar.preload_act_table_set("natural_log_exp_and_others")
            with act.Fori(0, 2) as i:
                for j in range(2):
                    slab_hi(j, i * (16 * SB_SLABS) + 64, i * SB_GROUPS + (G_SB + (sb_group("v", TT - 1) if j else
                                                                                 sb_group("v_first"))), full(SLAB))
                    for t in ((3,) if j else (0, 1, 2)):
                        store_value(i, t, G_SB + sb_group("v"), SB_GROUPS, "v_hi")
                sb_tmp = (lambda g: t_half[HD * (g % 2):HD * (g % 2) + HD, :])
                sb_sems = ("pv_rdy", "o_tmp", "o_add")

                def operand_hi(p, which):
                    act.wait_ge(s[which + "_t"], i * PAIRS + (p + 2))
                    act.wait_ge(s["z_rdy"], i * HALF + (2 * p + 1))
                    op = qop if which == "q" else kop
                    nc.scalar.activation(op[:, 0, 0, :], t_proj, ACT.Copy).then_inc(s[which + "_hi"], 1)

                def log_exp(g):
                    act.wait_ge(s["z_rdy"], i * HALF + (g + 2))
                    act.wait_ge(s["w_lo"], i * PH + max(2 * g - 1, 1))
                    for n, c in enumerate(PARTS):
                        e = prob[g % 2][:, c]
                        nc.scalar.activation(e, z_of(g)[:, c], ACT.Abs).then_inc(s["z_abs"], 1)
                        act.wait_ge(s["z_abs"], i * PH + (2 * g + n + 1))
                        nc.scalar.activation(e, e, ACT.Exp, scale=-1.0).then_inc(s["sp_exp"], 1)
                        act.wait_ge(s["sp_exp"], i * PH + (2 * g + n + 1))
                        nc.scalar.activation(e, e, ACT.Ln, bias=1.0).then_inc(s["sp_ln"], 1)

                def weights(g):
                    act.wait_ge(s["surv_rdy"], i * HALF + (g + 1))
                    for n, c in enumerate(PARTS):
                        nc.scalar.activation(prob[g % 2][:, c], z_of(g)[:, c], ACT.Exp).then_inc(s["w_exp"], 1)
                        act.wait_ge(s["w_exp"], i * PH + (2 * g + n + 2))
                        nc.scalar.activation(pr_hi[g % 2][:, c], prob[g % 2][:, c], ACT.Copy).then_inc(s["w_hi"], 1)

                operand_hi(0, "q")
                operand_hi(0, "k")
                for p in range(PAIRS):
                    a, b = 2 * p, 2 * p + 1
                    log_exp(a)
                    log_exp(b)
                    if p:
                        half_out(i, a - 1, sb_sems, sb_tmp)
                    if p < PAIRS - 1:
                        operand_hi(p + 1, "q")
                    weights(a)
                    if p:
                        pair_hi(i, p - 1, "o_add", "o_hi")
                    if p < PAIRS - 1:
                        operand_hi(p + 1, "k")
                    weights(b)
                    half_out(i, a, sb_sems, sb_tmp)
                half_out(i, HALF - 1, sb_sems, sb_tmp)
                pair_hi(i, PAIRS - 1, "o_add", "o_hi")

            def after_out(x_sem, phase, g, n_in, g0):
                for m in range(KT):
                    act.wait_ge(s[x_sem], m + 1)
                    prepare(m, phase, g)
                    if m in (1, 3):
                        slab_hi(m // 2, 16 * n_in[m // 2] + 64, g0 + m + 1, full(SLAB))
                    elif m in (5, 7):
                        mlp_slab_hi([n + 4 for n in n_in], g0 + KT, 0, (m - 5) // 2)

            act.wait_ge(s["o_lo"], 2 * PAIRS + 1)
            act.wait_ge(s["gain_in"], 16 * 7)
            act.dma_start(scr[0:1, 3, :].bitcast(I32), pos_in).then_inc(s["pos_landed"], 16)
            after_out("so_x", 1, G_MLP, (N_SBO, N_SBO), G_SBO)

            for steps_done, tab in ((8, sin_t), (16, cos_t)):
                act.wait_ge(s["rope_v"], steps_done)
                nc.scalar.activation(tab, tab, ACT.Sin).then_inc(s["rope_s"], 1)

            def mlp(layer, n_stat, n_in, g0, tail):
                m_s = mlp_s[layer]
                root(n_stat, r_tok[:])

                def hidden(i, q):
                    act.wait_ge(m_s["evac"], i * MLP_GROUPS + (4 + q + 1))
                    act.wait_ge(m_s["lo"], i * KT + max(q, 1))
                    nc.scalar.activation(scr[:, 6 + q % 2, :], scr[:, 4 + q % 2, :], ACT.Square).then_inc(m_s["sq"], 1)
                    act.wait_ge(m_s["sq"], i * KT + (q + 2))
                    nc.scalar.activation(u_hi[:, q, :], scr[:, 6 + q % 2, :], ACT.Copy).then_inc(m_s["hi"], 1)

                def first(i):
                    for q in range(KT):
                        hidden(i, q)
                        if q % 2:
                            mlp_slab_hi(n_in, g0, i, 2 + q // 2)

                with act.Fori(0, NFB - 1) as i:
                    first(i)
                    for j in range(6, 10):
                        mlp_slab_hi(n_in, g0, i, j)
                first(NFB - 1)
                for m in range(KT):
                    act.wait_ge(m_s["evac"], (NFB - 1) * MLP_GROUPS + 4 + KT + m + 1)
                    tail(m)
                    if m in (1, 3):
                        mlp_slab_hi(n_in, g0, NFB - 1, 6 + m // 2)

            def to_down(m):
                prepare(m, 2, G_KV)
                if m == 5:
                    slab_hi(0, 16 * N_DOWN + 32, G_DOWN - 2, full(SLAB))
                if m == 7:
                    slab_hi(1, 16 * N_DOWN + 32, G_DOWN, rope_parts)

            mlp(0, 1, (N_MLP0, N_MLP0), G_MLP0, to_down)
            for m in range(KT):
                nc.scalar.activation(u_hi[:, m, :], xT[:, m, :], ACT.Copy, scale=gcol(G_ATTN + KT + m))\
                    .then_inc(s["gq_hi"], 1)
            slab_hi(0, 16 * N_DOWN + 64, G_DOWN + KRT, full(SLAB))
            slab_hi(1, 16 * N_DOWN + 64, G_DOWN + KRT + 1, full(KT * P))
            root(2, r_tok[:])
            act.wait_ge(s["st_ps"], 2)
            def latent_parts(n):
                act.wait_ge(s["lat_u"], n + 1)
                if n == 3:
                    act.wait_ge(s["lat_add"], 1)
                dst = (tab_a[:], acc[:], tab_b[:], acc[:], scr[:, 4, :])[n]
                src = scr[:, (2, 3, 5, 6, 7)[n], :]
                nc.scalar.activation(dst, src, ACT.Square).then_inc(s["lat_sq"], 1)
                act.wait_ge(group, G_DOWN + KRT + 1)
                nc.scalar.activation(h_hi[:, n, :], src, ACT.Copy, scale=gcol(G_LKV + n)).then_inc(s["lat_hi"], 1)

            for n in range(4):
                latent_parts(n)
            act.wait_ge(s["kr_v"], 3)
            for b in range(2):
                nc.scalar.activation(kop[HD:P, b, 0, :], scr[HD:P, 4, :], ACT.Copy).then_inc(s["kr_hi"], 1)
            root(3, acc[:])
            root(4, r_col[:])
            latent_parts(4)
            root(5, tab_b[:])

            act.wait_ge(s["st_inv"], 3)
            with act.Fori(0, 2) as i:
                for t in range(TT):
                    store_value(i, t, G_MLA + mla_group("v"), MLA_GROUPS, "mv_hi")
                mla_tmp = (lambda g: scr[HD:P, 5 + g % 2, :])
                mla_sems = ("mpv_rdy", "mo_tmp", "mo_add")

                def key_hi(p):
                    act.wait_ge(s["mk_t"], i * HALF + (2 * p + 2))
                    act.wait_ge(s["mz_rdy"], i * HALF + (2 * p + 1))
                    nc.scalar.activation(kop[0:HD, :, 0, :], scr[0:HD, 5:7, :], ACT.Copy).then_inc(s["mk_hi"], 1)

                def query_hi(g):
                    act.wait_ge(s["mq_t"], i * HALF + (g + 2))
                    act.wait_ge(s["mz_rdy"], i * HALF + max(g, 1))
                    nc.scalar.activation(qop[:, g % 2, 0, :], r_tok[:], ACT.Copy).then_inc(s["mq_hi"], 1)

                def soft(g):
                    z, b = z_of(g), g % 2
                    for n, maxima in zip(BLOCKS, (1, 3, 3, 4)):
                        act.wait_ge(s["m_max"], i * (HALF * TT) + (TT * g + maxima))
                        c = slice(OFF[n], OFF[n] + WID[n])
                        nc.scalar.activation(prob[b][:, c], z[:, c], ACT.Exp, bias=nmax[:, b, n:n + 1],
                                             accum_out=rsum[:, b, n:n + 1]).then_inc(s["m_exp"], 1)

                def normalise(g):
                    b = g % 2
                    act.wait_ge(s["m_inv"], i * HALF + (g + 1))
                    for n in range(TT):
                        c = slice(OFF[n], OFF[n] + WID[n])
                        nc.scalar.activation(prob[b][:, c], prob[b][:, c], ACT.Copy, scale=rsum[:, b, n:n + 1])\
                            .then_inc(s["m_norm_b"], 1)

                def weight_hi(g):
                    act.wait_ge(s["mt_rdy"], i * HALF + (g + 1))
                    act.wait_ge(s["mpv_rdy"], i * HALF + max(g, 1))
                    for c in PARTS:
                        nc.scalar.activation(pr_hi[g % 2][:, c], z_of(g)[:, c], ACT.Copy).then_inc(s["mw_hi"], 1)

                key_hi(0)
                query_hi(0)
                query_hi(1)
                for p in range(PAIRS):
                    a, b = 2 * p, 2 * p + 1
                    more = p < PAIRS - 1
                    soft(a)
                    soft(b)
                    if more:
                        key_hi(p + 1)
                        normalise(b)
                    if p:
                        half_out(i, a - 1, mla_sems, mla_tmp)
                    if more:
                        query_hi(a + 2)
                    weight_hi(a)
                    if p:
                        pair_hi(i, p - 1, "mo_add", "mo_hi")
                    weight_hi(b)
                    if more:
                        query_hi(b + 2)
                    half_out(i, a, mla_sems, mla_tmp)
                half_out(i, HALF - 1, mla_sems, mla_tmp)
                pair_hi(i, PAIRS - 1, "mo_add", "mo_hi")

            after_out("mo_x", 3, G_MLP + KT, IN_MLAO, G_MLAO)

            def last_tail(m):
                square(m, 4)
                act.wait_ge(s["sq_done"], 3 * KT + m + 1)
                nc.scalar.activation(xT[:, m, :], xT[:, m, :], ACT.Copy, scale=gcol(G_FIN + m)).then_inc(s["f_xg"], 1)

            mlp(1, 6, IN_MLP1, G_MLP1, last_tail)
            root(7, r_col[:])
            act.wait_ge(s["st_inv"], 7)
            for t in range(TT):
                act.wait_ge(s["f_tr"], TT + t + 1)
                nc.scalar.activation(scf[:, t * D + T:(t + 1) * D], out_bank(1, t), ACT.Copy,
                                     scale=r_col[:, t:t + 1]).then_inc(s["f_out_s"], 1)

        @block.vector
        def _(dve):
            v = nc.vector
            start_at_one(dve, "q_t k_t q_lo k_lo w_lo o_add o_lo mk_lo mq_t mq_lo mw_lo mo_add mo_lo")
            for l in range(2):
                dve.sem_inc(mlp_s[l]["lo"], 1)

            def lower(m, phase, g):
                dve.wait_ge(s["h_hi"], phase * KT + m + 1)
                v.scalar_tensor_tensor(h_lo[:, m, :], xT[:, m, :], gcol(g + m), h_hi[:, m, :].bitcast(F32),
                                       ALU.mult, ALU.subtract).then_inc(s["h_lo"], 1)
                add_square(m, phase)

            def add_square(m, phase):
                if m:
                    dve.wait_ge(s["sq_done"], (phase - 1) * KT + m + 1)
                    dve.wait_ge(s["acc_add"], (phase - 1) * (KT - 1) + m - 1)
                    v.tensor_tensor(acc[:], acc[:], sq_tmp[m % 2][:], ALU.add).then_inc(s["acc_add"], 1)

            def mean(n, dst, src, width):
                dve.wait_ge(s["st_ps"], n)
                v.tensor_scalar(dst, src, 1.0 / width, EPS, ALU.mult, ALU.add).then_inc(s["st_var"], 1)

            def inverse(n, dst):
                dve.wait_ge(s["st_sqrt"], n)
                v.reciprocal(dst, dst).then_inc(s["st_inv"], 1)

            for m in range(KT):
                dve.wait_ge(s["xt_ready"], m + 1)
                v.tensor_copy(xT[:, m, :], banks[m]).then_inc(s["x_done"], 1)
                if m == 1:
                    dve.wait_ge(s["sum_sq"], TT)
                    v.tensor_scalar(r_col[:], r_col[:], 1.0 / D, EPS, ALU.mult, ALU.add).then_inc(s["r_var"], 1)
            dve.wait_ge(s["r_sqrt"], 1)
            v.reciprocal(r_col[:], r_col[:]).then_inc(s["r_inv"], 1)
            dve.wait_ge(s["r_inv"], 1)
            for t in range(TT):
                v.tensor_scalar(acc[:, t * P:(t + 1) * P], ident[:], r_col[:, t:t + 1], None, ALU.mult)\
                    .then_inc(s["diag"], 1)
            dve.wait_ge(s["gain0_in"], 16)
            for m in range(KT):
                dve.wait_ge(s["h_hi"], m + 1)
                v.scalar_tensor_tensor(h_lo[:, m, :], xT[:, m, :], gcol(G_ATTN + m), h_hi[:, m, :].bitcast(F32),
                                       ALU.mult, ALU.subtract).then_inc(s["h_lo"], 1)
            dve.wait_ge(s["const_cast"], 5)
            dve.wait_ge(s["r_row"], 1)
            v.tensor_copy(r_tok[:], po[:])
            v.tensor_scalar(tab_a[:], po[:], SB_SCALE, None, ALU.mult).then_inc(s["q_scale"], 1)
            dve.wait_ge(s["q_scale"], 1)

            def value_lo(i, hi_sem, lo_sem, tiles=range(TT)):
                for t in tiles:
                    dve.wait_ge(s[hi_sem], i * TT + (t + 1))
                    v.scalar_tensor_tensor(vst[:, t, :, 1, :], banks[t].rearrange("p (h c) -> p h c", c=HD),
                                           r_col[:, t:t + 1], vst[:, t, :, 0, :].bitcast(F32), ALU.mult,
                                           ALU.subtract).then_inc(s[lo_sem], 1)

            def add_out(i, g, sems, tmp):
                o_tmp, o_add, o_lo = sems
                dve.wait_ge(s[o_tmp], i * HALF + (g + 1))
                dve.wait_ge(s[o_lo], i * PAIRS + (g // 2 + 1))
                r = slice(HD * (g % 2), HD * (g % 2) + HD)
                v.tensor_tensor(t_out[r, :], po[0:HD, :], tmp(g), ALU.add).then_inc(s[o_add], 1)

            def pair_lo(i, p, o_hi, o_lo, o_add):
                dve.wait_ge(s[o_hi], i * PAIRS + (p + 1))
                v.tensor_tensor(u_lo[:, i * PAIRS + p, :], t_out, u_hi[:, i * PAIRS + p, :].bitcast(F32),
                                ALU.subtract).then_inc(s[o_lo], 1)

            with dve.Fori(0, 2) as i:
                value_lo(i, "v_hi", "v_lo")
                sb_tmp = (lambda g: t_half[HD * (g % 2):HD * (g % 2) + HD, :])
                sb_sems = ("o_tmp", "o_add", "o_lo")

                def scale(p, which):
                    dve.wait_ge(group, i * SB_GROUPS + (G_SB + sb_group(which, p)))
                    if which == "q":
                        dve.wait_ge(s["k_lo"], i * PAIRS + (p + 1))
                    else:
                        dve.wait_ge(s["q_lo"], i * PAIRS + (p + 2))
                    bank = po if which == "k" and p == 0 else pj
                    v.tensor_tensor(t_proj, bank[:], (tab_a if which == "q" else r_tok)[:], ALU.mult)\
                        .then_inc(s[which + "_t"], 1)

                def operand_lo(p, which):
                    op = qop if which == "q" else kop
                    dve.wait_ge(s[which + "_hi"], i * PAIRS + (p + 1))
                    v.tensor_tensor(op[:, 0, 1, :], t_proj, op[:, 0, 0, :].bitcast(F32), ALU.subtract)\
                        .then_inc(s[which + "_lo"], 1)

                def softplus(g):
                    for n, c in enumerate(PARTS):
                        e, count = prob[g % 2][:, c], 2 * g + n + 1
                        dve.wait_ge(s["sp_ln"], i * PH + count)
                        v.scalar_tensor_tensor(e, z_of(g)[:, c], 0.0, e, ALU.max, ALU.add).then_inc(s["sp_sum"], 1)
                        dve.wait_ge(s["sp_sum"], i * PH + count)
                        if n == 0:
                            dve.wait_ge(s["pv_rdy"], i * HALF + max(g, 1))
                        v.tensor_copy(pr_hi[g % 2][:, c], e).then_inc(s["sp_hi"], 1)
                        dve.wait_ge(s["sp_hi"], i * PH + count)
                        v.tensor_tensor(pr_lo[g % 2][:, c], e, pr_hi[g % 2][:, c].bitcast(F32), ALU.subtract)\
                            .then_inc(s["sp_lo"], 1)

                def weight_lo(g):
                    for n, c in enumerate(PARTS):
                        dve.wait_ge(s["w_hi"], i * PH + (2 * g + n + 1))
                        v.tensor_tensor(pr_lo[g % 2][:, c], prob[g % 2][:, c], pr_hi[g % 2][:, c].bitcast(F32),
                                        ALU.subtract).then_inc(s["w_lo"], 1)

                scale(0, "q")
                operand_lo(0, "q")
                scale(0, "k")
                operand_lo(0, "k")
                for p in range(PAIRS):
                    a, b = 2 * p, 2 * p + 1
                    more = p < PAIRS - 1
                    softplus(a)
                    if more:
                        scale(p + 1, "q")
                    softplus(b)
                    if p:
                        add_out(i, a - 1, sb_sems, sb_tmp)
                    if more:
                        operand_lo(p + 1, "q")
                    weight_lo(a)
                    if p:
                        pair_lo(i, p - 1, "o_hi", "o_lo", "o_add")
                    if more:
                        scale(p + 1, "k")
                        operand_lo(p + 1, "k")
                    weight_lo(b)
                    add_out(i, a, sb_sems, sb_tmp)
                add_out(i, HALF - 1, sb_sems, sb_tmp)
                pair_lo(i, PAIRS - 1, "o_hi", "o_lo", "o_add")

            def add_x(m, bank, count, sem):
                dve.wait_ge(group, count)
                v.tensor_tensor(xT[:, m, :], bank, xT[:, m, :], ALU.add).then_inc(sem, 1)

            def after_out(g0, x_sem, phase, g, between):
                for m in range(KT):
                    add_x(m, banks[m % 4], g0 + m + 1, s[x_sem])
                    if m:
                        lower(m - 1, phase, g)
                    between(m)
                lower(KT - 1, phase, g)

            steps = [0]

            def step(ins):
                steps[0] += 1
                ins.then_inc(s["rope_v"], 1)
                dve.wait_ge(s["rope_v"], steps[0])

            ang, turns = scr[:, 2, :], scr[:, 3, :]

            def angle():
                dve.wait_ge(s["rope_ps"], 1)
                step(v.tensor_scalar(ang, pj[:], cols[:, COL_FREQ:COL_FREQ + 1], None, ALU.mult))

            def reduced(tab, quarter):
                step(v.tensor_scalar(turns, ang, 1.0 / TWO_PI, quarter, ALU.mult, ALU.add))
                step(v.tensor_scalar(turns, turns, ROUNDER, None, ALU.add))
                step(v.tensor_scalar(turns, turns, ROUNDER, None, ALU.subtract))
                step(v.scalar_tensor_tensor(tab, turns, -PI_A, ang, ALU.mult, ALU.add))
                step(v.scalar_tensor_tensor(tab, turns, -PI_B, tab, ALU.mult, ALU.add))
                step(v.scalar_tensor_tensor(tab, turns, -PI_C, tab, ALU.mult, ALU.add))
                if quarter:
                    step(v.tensor_scalar(tab, tab, TWO_PI * quarter, None, ALU.add))
                step(v.tensor_scalar(tab, tab, PI_SAFE, -PI_SAFE, ALU.min, ALU.max))

            def rotary(m):
                if m == 0:
                    dve.wait_ge(s["pos_landed"], 16)
                    v.tensor_copy(scr[0:1, 0, :], scr[0:1, 3, :].bitcast(I32)).then_inc(s["rope_pos"], 1)
                elif m == 4:
                    angle()
                    reduced(sin_t, 0.0)
                elif m == 6:
                    reduced(cos_t, 0.25)

            after_out(G_SBO, "so_x", 1, G_MLP, rotary)

            def mlp(layer, g0, n_stat, tail):
                m_s = mlp_s[layer]
                mean(n_stat, r_tok[:], po[:], D)
                inverse(n_stat, r_tok[:])
                dve.wait_ge(s["st_inv"], n_stat)

                def relu(i, q):
                    dve.wait_ge(group, i * MLP_GROUPS + (g0 + q + 1))
                    dve.wait_ge(m_s["sq"], i * KT + max(q, 1))
                    v.scalar_tensor_tensor(scr[:, 4 + q % 2, :], banks[q % 4], 0.0, r_tok[:], ALU.max, ALU.mult)\
                        .then_inc(m_s["evac"], 1)

                def hidden_lo(i, q):
                    dve.wait_ge(m_s["hi"], i * KT + (q + 1))
                    v.tensor_tensor(u_lo[:, q, :], scr[:, 6 + q % 2, :], u_hi[:, q, :].bitcast(F32), ALU.subtract)\
                        .then_inc(m_s["lo"], 1)

                def first(i):
                    for q in range(KT):
                        relu(i, q)
                        if q:
                            hidden_lo(i, q - 1)
                    hidden_lo(i, KT - 1)

                with dve.Fori(0, NFB - 1) as i:
                    first(i)
                    for m in range(KT):
                        add_x(m, banks[m % 4], i * MLP_GROUPS + (g0 + KT + m + 1), m_s["evac"])
                first(NFB - 1)
                for m in range(KT):
                    add_x(m, banks[m % 4], (NFB - 1) * MLP_GROUPS + g0 + KT + m + 1, m_s["evac"])
                    if m:
                        tail(m - 1)
                tail(KT - 1)

            mlp(0, G_MLP0, 1, lambda m: lower(m, 2, G_KV))
            for m in range(KT):
                dve.wait_ge(s["gq_hi"], m + 1)
                v.scalar_tensor_tensor(u_lo[:, m, :], xT[:, m, :], gcol(G_ATTN + KT + m), u_hi[:, m, :].bitcast(F32),
                                       ALU.mult, ALU.subtract).then_inc(s["gq_lo"], 1)
            mean(2, r_tok[:], po[:], D)
            inverse(2, r_tok[:])
            dve.wait_ge(s["st_inv"], 2)

            lat_tile = (2, 3, 5, 6, 7)
            lat_bank = (0, 1, 3, 4, 5)

            def latent(n):
                dve.wait_ge(group, G_DOWN + lat_bank[n] + 1)
                v.tensor_tensor(scr[:, lat_tile[n], :], banks[lat_bank[n]], r_tok[:], ALU.mult)\
                    .then_inc(s["lat_u"], 1)

            def latent_lo(n):
                dve.wait_ge(s["lat_hi"], n + 1)
                v.scalar_tensor_tensor(h_lo[:, n, :], scr[:, lat_tile[n], :], gcol(G_LKV + n),
                                       h_hi[:, n, :].bitcast(F32), ALU.mult, ALU.subtract).then_inc(s["lat_lo"], 1)

            def latent_add(n, dst, src, count):
                dve.wait_ge(s["lat_sq"], n + 1)
                dve.wait_ge(s["lat_add"], count)
                v.tensor_tensor(dst[:], dst[:], src, ALU.add).then_inc(s["lat_add"], 1)

            latent(0)
            latent(1)
            latent_add(1, tab_a, acc[:], 0)
            dve.wait_ge(group, G_DOWN + KRT + 1)
            v.tensor_tensor(scr[:, 4, :], banks[2], r_tok[:], ALU.mult).then_inc(s["ra_u"], 1)
            latent_lo(0)
            latent_lo(1)
            latent(2)
            latent_lo(2)
            latent(3)
            latent_add(3, tab_b, acc[:], 1)
            latent_lo(3)
            dve.wait_ge(s["rope_s"], 2)
            dve.wait_ge(s["rb_ps"], 1)
            v.tensor_tensor(scr[:, 4, :], scr[:, 4, :], cos_t, ALU.mult).then_inc(s["kr_v"], 1)
            v.tensor_tensor(scr[:, 7, :], pj[:], sin_t, ALU.mult).then_inc(s["kr_v"], 1)
            dve.wait_ge(s["kr_v"], 2)
            v.tensor_tensor(scr[:, 4, :], scr[:, 4, :], scr[:, 7, :], ALU.add).then_inc(s["kr_v"], 1)
            mean(3, acc[:], po[:], KR)
            mean(4, r_col[:], banks[0][:, 0:TT], KR)
            v.tensor_scalar(tab_a[:], cos_t, cols[:, COL_COS:COL_COS + 1], cols[:, COL_ONE:COL_ONE + 1],
                            ALU.mult, ALU.add).then_inc(s["tab_v"], 1)
            for b in range(2):
                dve.wait_ge(s["kr_hi"], b + 1)
                ins = v.tensor_tensor(kop[HD:P, b, 1, :], scr[HD:P, 4, :], kop[HD:P, b, 0, :].bitcast(F32),
                                      ALU.subtract)
            ins.then_inc(s["kr_lo"], 1)
            dve.wait_ge(s["tab_v"], 1)
            v.scalar_tensor_tensor(tab_a[:], sin_t, cols[:, COL_SIN:COL_SIN + 1], tab_a[:], ALU.mult, ALU.add)\
                .then_inc(s["tab_v"], 1)
            latent(4)
            inverse(4, r_col[:])
            latent_add(4, tab_b, scr[:, 4, :], 2)
            latent_lo(4)
            inverse(3, acc[:])
            mean(5, tab_b[:], pj[:], QR)
            inverse(5, tab_b[:])
            dve.wait_ge(s["tab_v"], 2)
            dve.wait_ge(s["st_inv"], 5)
            v.tensor_tensor(tab_a[:], tab_a[:], tab_b[:], ALU.mult).then_inc(s["tab_v"], 1)
            dve.wait_ge(s["tab_v"], 3)

            with dve.Fori(0, 2) as i:
                mla_tmp = (lambda g: scr[HD:P, 5 + g % 2, :])
                mla_sems = ("mo_tmp", "mo_add", "mo_lo")

                def key(p):
                    dve.wait_ge(group, i * MLA_GROUPS + (G_MLA + mla_group("k", p)))
                    dve.wait_ge(s["mk_lo"], i * PAIRS + (p + 1))
                    for b in range(2):
                        r = slice(HD * b, HD * b + HD)
                        v.tensor_tensor(scr[0:HD, 5 + b, :], pj[r, :], acc[r, :], ALU.mult).then_inc(s["mk_t"], 1)

                def key_lo(p):
                    dve.wait_ge(s["mk_hi"], i * PAIRS + (p + 1))
                    v.tensor_tensor(kop[0:HD, :, 1, :], scr[0:HD, 5:7, :], kop[0:HD, :, 0, :].bitcast(F32),
                                    ALU.subtract).then_inc(s["mk_lo"], 1)

                def query(g):
                    dve.wait_ge(group, i * MLA_GROUPS + (G_MLA + mla_group("q", g)))
                    dve.wait_ge(s["mq_lo"], i * HALF + (g + 1))
                    v.tensor_tensor(r_tok[:], po[:] if g == 0 else pj[:], tab_a[:], ALU.mult).then_inc(s["mq_t"], 1)

                def query_lo(g):
                    dve.wait_ge(s["mq_hi"], i * HALF + (g + 1))
                    v.tensor_tensor(qop[:, g % 2, 1, :], r_tok[:], qop[:, g % 2, 0, :].bitcast(F32), ALU.subtract)\
                        .then_inc(s["mq_lo"], 1)

                def row_max(g):
                    dve.wait_ge(s["mz_rdy"], i * HALF + (g + 2))
                    z = z_of(g)
                    for n in BLOCKS:
                        v.tensor_reduce(nmax[:, g % 2, n:n + 1], z[:, OFF[n]:OFF[n] + WID[n]], AX.X, ALU.max,
                                        negate=True).then_inc(s["m_max"], 1)

                def sum_inverse(g):
                    dve.wait_ge(s["m_exp"], i * (HALF * TT) + TT * (g + 1))
                    v.reciprocal(rsum[:, g % 2, :], rsum[:, g % 2, :]).then_inc(s["m_inv"], 1)

                def normalise(g):
                    b = g % 2
                    dve.wait_ge(s["m_inv"], i * HALF + (g + 1))
                    for n in range(TT):
                        c = slice(OFF[n], OFF[n] + WID[n])
                        v.tensor_scalar(prob[b][:, c], prob[b][:, c], rsum[:, b, n:n + 1], None, ALU.mult)\
                            .then_inc(s["m_norm_b" if b else "m_norm"], 1)

                def weight_lo(g):
                    for n, c in enumerate(PARTS):
                        dve.wait_ge(s["mw_hi"], i * PH + (2 * g + n + 1))
                        v.tensor_tensor(pr_lo[g % 2][:, c], z_of(g)[:, c], pr_hi[g % 2][:, c].bitcast(F32),
                                        ALU.subtract).then_inc(s["mw_lo"], 1)

                value_lo(i, "mv_hi", "mv_lo", range(TT - 1))
                key(0)
                value_lo(i, "mv_hi", "mv_lo", (TT - 1,))
                key_lo(0)
                query(0)
                query_lo(0)
                query(1)
                query_lo(1)
                for p in range(PAIRS):
                    a, b = 2 * p, 2 * p + 1
                    more = p < PAIRS - 1
                    row_max(a)
                    row_max(b)
                    if more:
                        key(p + 1)
                    sum_inverse(a)
                    normalise(a)
                    sum_inverse(b)
                    if more:
                        key_lo(p + 1)
                        query(a + 2)
                    if p:
                        add_out(i, a - 1, mla_sems, mla_tmp)
                    if not more:
                        normalise(b)
                    weight_lo(a)
                    if more:
                        query_lo(a + 2)
                    weight_lo(b)
                    if more:
                        query(b + 2)
                    if p:
                        pair_lo(i, p - 1, "mo_hi", "mo_lo", "mo_add")
                    if more:
                        query_lo(b + 2)
                    add_out(i, a, mla_sems, mla_tmp)
                add_out(i, HALF - 1, mla_sems, mla_tmp)
                pair_lo(i, PAIRS - 1, "mo_hi", "mo_lo", "mo_add")

            after_out(G_MLAO, "mo_x", 3, G_MLP + KT, lambda m: None)
            mlp(1, G_MLP1, 6, lambda m: add_square(m, 4))
            mean(7, r_col[:], pj[:, 0:TT], D)
            inverse(7, r_col[:])
            dve.wait_ge(s["st_inv"], 7)
            for t in range(TT):
                dve.wait_ge(s["f_tr"], t + 1)
                v.tensor_scalar(scf[:, t * D:t * D + T], out_bank(0, t), r_col[:, t:t + 1], None, ALU.mult)\
                    .then_inc(s["f_out_v"], 1)


_INS = ["x", "positions", "attn_norm", "mlp_norm", "sb_w_qkv", "sb_w_o", "kv_norm", "mla_w_dkv", "mla_kv_lat_norm",
        "mla_w_ukv", "mla_w_dq", "mla_q_lat_norm", "mla_w_uq", "mla_w_o", "mlp_w1", "mlp_w2", "final_norm"]


def kernel(**inputs):
    import numpy as _np
    import concourse.bacc as _bacc
    from concourse import mybir as _mybir
    from concourse.bass_utils import run_bass_kernel_spmd as _run

    nc = _bacc.Bacc("TRN2", target_bir_lowering=False, num_devices=1)
    arrays, args = {}, []
    for name in _INS:
        a = _np.ascontiguousarray(inputs[name])
        arrays[f"in_{name}_dram"] = a
        args.append(nc.dram_tensor(f"in_{name}_dram", a.shape, _mybir.dt.from_np(a.dtype), kind="ExternalInput").ap())
    c = constants()
    arrays["in_consts_dram"] = c
    args.append(nc.dram_tensor("in_consts_dram", c.shape, _mybir.dt.float32, kind="ExternalInput").ap())
    args.append(nc.dram_tensor("out_0_dram", (1, T, D), _mybir.dt.float32, kind="ExternalOutput").ap())
    build(nc, *args)
    r = _run(nc, [arrays], core_ids=[0])
    return r.results[0]["out_0_dram"]
```
